# Optimizing a Trainium2 kernel written in Bass

```python
import math
import jax
import jax.numpy as jnp
from jax import lax
import numpy as np

D_MODEL = 1024
BATCH = 1
SEQ = 512
DEPTH = 1
DEC_BATCH = 8
DEC_SEQ = 1
PAST_LEN = 2048
PAGE_SIZE = 128

HEAD_DIM = 64
CONV_W = D_MODEL // 2
CONV_K = 3
SB_HEADS = D_MODEL // 128
SB_W = SB_HEADS * HEAD_DIM
SB_BLOCK = 128
SB_BIAS_INIT = -6.0
DIL_GROUPS = ((128, 1), (512, 4), (2048, 16))
DIL_HEADS_PER_GROUP = D_MODEL // 256
DIL_HEADS = DIL_HEADS_PER_GROUP * len(DIL_GROUPS)
DIL_W = DIL_HEADS * HEAD_DIM
DIL_OUT = DIL_HEADS_PER_GROUP * HEAD_DIM
DIL_SPAN = 128
D_FF = 4 * D_MODEL
REL_BUCKETS = 32
REL_MAX_EXACT = 16
REL_MAX_DIST = 2048
N_BRANCH = 3
RMS_EPS = 1e-6
SPLIT_SIZES = (CONV_W,) * 3 + (SB_W,) * 3 + (DIL_W,) * 3 + (D_MODEL,) * N_BRANCH
N_IN = sum(SPLIT_SIZES)
SPLIT_POINTS = tuple(int(s) for s in np.cumsum(SPLIT_SIZES)[:-1])

kernel_name = "hybrid_conv_stickbreak_dilated_decoder_step"

def rmsnorm(x, g):
    xf = x.astype(jnp.float32)
    xf = xf * lax.rsqrt(jnp.mean(xf * xf, axis=-1, keepdims=True) + RMS_EPS)
    return (xf * g.astype(jnp.float32)).astype(x.dtype)

def rel_bucket(dist):
    n = jnp.maximum(dist, 0)
    nf = jnp.maximum(n, 1).astype(jnp.float32)
    large = REL_MAX_EXACT + (jnp.log(nf / REL_MAX_EXACT) / math.log(REL_MAX_DIST / REL_MAX_EXACT)
                             * (REL_BUCKETS - REL_MAX_EXACT)).astype(jnp.int32)
    large = jnp.minimum(large, REL_BUCKETS - 1)
    return jnp.where(n < REL_MAX_EXACT, n, large)

def in_projection(h, norm_g, w_in, b_gate):
    xn = rmsnorm(h, norm_g)
    parts = jnp.split(xn @ w_in, SPLIT_POINTS, axis=-1)
    gates = tuple(jax.nn.sigmoid(parts[9 + i] + b_gate[i]) for i in range(N_BRANCH))
    return parts[0:3], parts[3:6], parts[6:9], gates

def conv_mixer(parts, prev_rows, conv_w, w_branch):
    gate_b, gate_c, h_in = parts
    u = gate_c * h_in
    t = u.shape[1]
    u_ext = jnp.concatenate([prev_rows.astype(u.dtype), u], axis=1)
    y = u_ext[:, 0:t] * conv_w[0]
    for i in range(1, CONV_K):
        y = y + u_ext[:, i:i + t] * conv_w[i]
    return (gate_b * y) @ w_branch, u_ext[:, t:]

def sb_block(q, k, v, q_pos, k_pos, b_sb):
    z = (jnp.einsum('bqhd,bkhd->bhqk', q, k).astype(jnp.float32) * (HEAD_DIM ** -0.5)
         + b_sb.astype(jnp.float32)[None, :, None, None])
    valid = k_pos[None, :] < q_pos[:, None]
    log_keep = jnp.where(valid, jax.nn.log_sigmoid(-z), 0.0)
    after = lax.cumsum(log_keep, axis=3, reverse=True) - log_keep
    a = jnp.where(valid, jnp.exp(jax.nn.log_sigmoid(z) + after), 0.0)
    return jnp.einsum('bhqk,bkhd->bqhd', a.astype(v.dtype), v)

def sb_attention(q, k, v, q_pos, k_pos, b_sb):
    b, t, h, dh = q.shape
    bq = min(SB_BLOCK, t)
    nb = t // bq
    qb = q.reshape(b, nb, bq, h, dh).transpose(1, 0, 2, 3, 4)
    pb = q_pos.reshape(nb, bq)
    o = lax.map(lambda xs: sb_block(xs[0], k, v, xs[1], k_pos, b_sb), (qb, pb))
    return o.transpose(1, 0, 2, 3, 4).reshape(b, t, h, dh)

def dilated_prompt_group(q, k, v, bias_tab, dil):
    b, s, h, dh = q.shape
    L = s // dil
    nb = -(-L // DIL_SPAN)
    lp = nb * DIL_SPAN
    bn = b * dil

    def sub(a):
        return a.reshape(b, L, dil, h, dh).transpose(0, 2, 1, 3, 4).reshape(bn, L, h, dh)

    qs = jnp.pad(sub(q), ((0, 0), (0, lp - L), (0, 0), (0, 0))).reshape(bn, nb, DIL_SPAN, h, dh)

    def key_blocks(a):
        ap = jnp.pad(sub(a), ((0, 0), (DIL_SPAN, lp - L), (0, 0), (0, 0)))
        prev = ap[:, :lp].reshape(bn, nb, DIL_SPAN, h, dh)
        cur = ap[:, DIL_SPAN:].reshape(bn, nb, DIL_SPAN, h, dh)
        return jnp.concatenate([prev, cur], axis=2)

    kb, vb = key_blocks(k), key_blocks(v)
    qi = jnp.arange(DIL_SPAN)[:, None]
    ki = jnp.arange(2 * DIL_SPAN)[None, :]
    dist = DIL_SPAN + qi - ki
    key_idx = jnp.arange(nb)[:, None, None] * DIL_SPAN + ki[None] - DIL_SPAN
    valid = (dist >= 0) & (dist <= DIL_SPAN) & (key_idx >= 0)
    bias = bias_tab[rel_bucket(dist * dil)].astype(jnp.float32).transpose(2, 0, 1)
    logits = jnp.einsum('nbqhd,nbkhd->nbhqk', qs, kb).astype(jnp.float32) * (HEAD_DIM ** -0.5) + bias
    logits = jnp.where(valid[None, :, None], logits, -jnp.inf)
    lse = jax.nn.logsumexp(logits, axis=-1)
    p = jnp.exp(logits - lse[..., None])
    o = jnp.einsum('nbhqk,nbkhd->nbqhd', p.astype(v.dtype), vb)
    o = o.reshape(bn, lp, h, dh)[:, :L].reshape(b, dil, L, h, dh).transpose(0, 2, 1, 3, 4).reshape(b, s, h, dh)
    lse = lse.transpose(0, 1, 3, 2).reshape(bn, lp, h)[:, :L].reshape(b, dil, L, h).transpose(0, 2, 1, 3).reshape(b, s, h)
    return o, lse

def dilated_sample_group(q, k_new, v_new, k_buf, v_buf, bias_tab, dil, window):
    t = q.shape[1]
    lb = k_buf.shape[1]
    kk = jnp.concatenate([k_buf, k_new], axis=1)
    vv = jnp.concatenate([v_buf, v_new], axis=1)
    steps = jnp.arange(DIL_SPAN + 1)
    idx = lb + jnp.arange(t)[:, None] - steps[None, :] * dil
    valid = idx >= 0
    idx_c = jnp.maximum(idx, 0)
    kg = kk[:, idx_c]
    vg = vv[:, idx_c]
    bias = bias_tab[rel_bucket(steps * dil)].astype(jnp.float32).T
    logits = jnp.einsum('bthd,btjhd->bhtj', q, kg).astype(jnp.float32) * (HEAD_DIM ** -0.5) + bias[:, None, :]
    logits = jnp.where(valid[None, None], logits, -jnp.inf)
    lse = jax.nn.logsumexp(logits, axis=-1)
    p = jnp.exp(logits - lse[..., None])
    o = jnp.einsum('bhtj,btjhd->bthd', p.astype(vg.dtype), vg)
    keep = min(window, kk.shape[1])
    return o, lse.transpose(0, 2, 1), kk[:, kk.shape[1] - keep:], vv[:, vv.shape[1] - keep:]

def combine_groups(outs, lses, dtype):
    w = jax.nn.softmax(jnp.stack(lses, axis=0), axis=0)
    o = jnp.sum(w[..., None] * jnp.stack(outs, axis=0).astype(jnp.float32), axis=0)
    return o.astype(dtype)

def merge_and_mlp(h, gates, y_a, y_b, y_c, w_out, norm_mlp_g, w_up, w_down):
    mixed = gates[0] * y_a + gates[1] * y_b + gates[2] * y_c
    h = h + mixed @ w_out
    hn = rmsnorm(h, norm_mlp_g)
    return h + jnp.square(jax.nn.relu(hn @ w_up)) @ w_down

def gather_pages(pool, page_table):
    g = pool[page_table]
    return g.reshape(g.shape[0], g.shape[1] * g.shape[2], g.shape[3], g.shape[4])

def layer_prompt(h, p, rel_bias):
    (norm_mix_g, w_in, b_gate, conv_w, w_br_conv, w_br_sb, b_sb, w_br_dil,
     w_out, norm_mlp_g, w_up, w_down) = p
    bsz, s, _ = h.shape
    conv_parts, sb_parts, dil_parts, gates = in_projection(h, norm_mix_g, w_in, b_gate)
    zeros = jnp.zeros((bsz, CONV_K - 1, CONV_W), h.dtype)
    y_a, conv_rows = conv_mixer(conv_parts, zeros, conv_w, w_br_conv)
    q, k, v = (a.reshape(bsz, s, SB_HEADS, HEAD_DIM) for a in sb_parts)
    pos = jnp.arange(s)
    y_b = sb_attention(q, k, v, pos, pos, b_sb).reshape(bsz, s, SB_W) @ w_br_sb
    qd, kd, vd = (a.reshape(bsz, s, DIL_HEADS, HEAD_DIM) for a in dil_parts)
    outs, lses, win_k, win_v = [], [], [], []
    for g, (window, dil) in enumerate(DIL_GROUPS):
        heads = slice(g * DIL_HEADS_PER_GROUP, (g + 1) * DIL_HEADS_PER_GROUP)
        o, lse = dilated_prompt_group(qd[:, :, heads], kd[:, :, heads], vd[:, :, heads], rel_bias[:, heads], dil)
        outs.append(o)
        lses.append(lse)
        keep = min(window, s)
        win_k.append(kd[:, s - keep:, heads])
        win_v.append(vd[:, s - keep:, heads])
    y_c = combine_groups(outs, lses, h.dtype).reshape(bsz, s, DIL_OUT) @ w_br_dil
    h = merge_and_mlp(h, gates, y_a, y_b, y_c, w_out, norm_mlp_g, w_up, w_down)
    return h, k, v, win_k, win_v, conv_rows

def layer_sample(h, p, rel_bias, pool_k, pool_v, page_table, win_k, win_v, conv_state):
    (norm_mix_g, w_in, b_gate, conv_w, w_br_conv, w_br_sb, b_sb, w_br_dil,
     w_out, norm_mlp_g, w_up, w_down) = p
    bsz, t, _ = h.shape
    conv_parts, sb_parts, dil_parts, gates = in_projection(h, norm_mix_g, w_in, b_gate)
    y_a, conv_rows = conv_mixer(conv_parts, conv_state, conv_w, w_br_conv)
    q, k, v = (a.reshape(bsz, t, SB_HEADS, HEAD_DIM) for a in sb_parts)
    k_all = jnp.concatenate([gather_pages(pool_k, page_table).astype(k.dtype), k], axis=1)
    v_all = jnp.concatenate([gather_pages(pool_v, page_table).astype(v.dtype), v], axis=1)
    past = k_all.shape[1] - t
    k_pos = jnp.arange(past + t)
    q_pos = past + jnp.arange(t)
    y_b = sb_attention(q, k_all, v_all, q_pos, k_pos, b_sb).reshape(bsz, t, SB_W) @ w_br_sb
    qd, kd, vd = (a.reshape(bsz, t, DIL_HEADS, HEAD_DIM) for a in dil_parts)
    outs, lses, new_k, new_v = [], [], [], []
    for g, (window, dil) in enumerate(DIL_GROUPS):
        heads = slice(g * DIL_HEADS_PER_GROUP, (g + 1) * DIL_HEADS_PER_GROUP)
        o, lse, kb, vb = dilated_sample_group(qd[:, :, heads], kd[:, :, heads], vd[:, :, heads],
                                              win_k[g].astype(kd.dtype), win_v[g].astype(vd.dtype),
                                              rel_bias[:, heads], dil, window)
        outs.append(o)
        lses.append(lse)
        new_k.append(kb)
        new_v.append(vb)
    y_c = combine_groups(outs, lses, h.dtype).reshape(bsz, t, DIL_OUT) @ w_br_dil
    h = merge_and_mlp(h, gates, y_a, y_b, y_c, w_out, norm_mlp_g, w_up, w_down)
    return h, k, v, new_k, new_v, conv_rows

def setup_inputs(seed: int = 0) -> dict:
    key = jax.random.key(seed)
    keys = iter(jax.random.split(key, 32))
    f32 = jnp.float32

    def normal(shape, scale):
        return jax.random.normal(next(keys), shape, f32) * scale

    n_pages = PAST_LEN // PAGE_SIZE
    n_used = DEC_BATCH * n_pages
    n_pool = n_used + (n_used + 3) // 4
    wl = [min(w, PAST_LEN) for w, _ in DIL_GROUPS]
    hg = DIL_HEADS_PER_GROUP
    return {
        'x_prompt': normal((BATCH, SEQ, D_MODEL), 1.0),
        'x_sample': normal((DEC_BATCH, DEC_SEQ, D_MODEL), 1.0),
        'cache_sb_k': normal((DEPTH, n_pool, PAGE_SIZE, SB_HEADS, HEAD_DIM), 1.0),
        'cache_sb_v': normal((DEPTH, n_pool, PAGE_SIZE, SB_HEADS, HEAD_DIM), 1.0),
        'cache_win128_k': normal((DEPTH, DEC_BATCH, wl[0], hg, HEAD_DIM), 1.0),
        'cache_win128_v': normal((DEPTH, DEC_BATCH, wl[0], hg, HEAD_DIM), 1.0),
        'cache_win512_k': normal((DEPTH, DEC_BATCH, wl[1], hg, HEAD_DIM), 1.0),
        'cache_win512_v': normal((DEPTH, DEC_BATCH, wl[1], hg, HEAD_DIM), 1.0),
        'cache_win2048_k': normal((DEPTH, DEC_BATCH, wl[2], hg, HEAD_DIM), 1.0),
        'cache_win2048_v': normal((DEPTH, DEC_BATCH, wl[2], hg, HEAD_DIM), 1.0),
        'state_conv': normal((DEPTH, DEC_BATCH, CONV_K - 1, CONV_W), 1.0),
        'page_table': jax.random.permutation(next(keys), n_pool)[:n_used].reshape(DEC_BATCH, n_pages).astype(jnp.int32),
        'norm_mix_g': 1.0 + normal((DEPTH, D_MODEL), 0.02),
        'w_in': normal((DEPTH, D_MODEL, N_IN), D_MODEL ** -0.5),
        'b_gate': normal((DEPTH, N_BRANCH, D_MODEL), 0.1),
        'conv_w': normal((DEPTH, CONV_K, CONV_W), CONV_K ** -0.5),
        'w_branch_conv': normal((DEPTH, CONV_W, D_MODEL), CONV_W ** -0.5),
        'w_branch_sb': normal((DEPTH, SB_W, D_MODEL), SB_W ** -0.5),
        'b_sb': SB_BIAS_INIT + normal((DEPTH, SB_HEADS), 0.1),
        'w_branch_dil': normal((DEPTH, DIL_OUT, D_MODEL), DIL_OUT ** -0.5),
        'w_out': normal((DEPTH, D_MODEL, D_MODEL), D_MODEL ** -0.5),
        'norm_mlp_g': 1.0 + normal((DEPTH, D_MODEL), 0.02),
        'w_mlp_up': normal((DEPTH, D_MODEL, D_FF), D_MODEL ** -0.5),
        'w_mlp_down': normal((DEPTH, D_FF, D_MODEL), D_FF ** -0.5),
        'rel_bias': normal((REL_BUCKETS, DIL_HEADS), 0.2),
        'norm_final_g': 1.0 + normal((D_MODEL,), 0.02),
    }

def reference(x_prompt, x_sample, cache_sb_k, cache_sb_v, cache_win128_k, cache_win128_v,
              cache_win512_k, cache_win512_v, cache_win2048_k, cache_win2048_v, state_conv,
              page_table, norm_mix_g, w_in, b_gate, conv_w, w_branch_conv, w_branch_sb, b_sb,
              w_branch_dil, w_out, norm_mlp_g, w_mlp_up, w_mlp_down, rel_bias, norm_final_g):
    params = (norm_mix_g, w_in, b_gate, conv_w, w_branch_conv, w_branch_sb, b_sb, w_branch_dil,
              w_out, norm_mlp_g, w_mlp_up, w_mlp_down)
    win_k_cache = (cache_win128_k, cache_win512_k, cache_win2048_k)
    win_v_cache = (cache_win128_v, cache_win512_v, cache_win2048_v)
    n_groups = len(DIL_GROUPS)
    h_p, h_s = x_prompt, x_sample
    sbk_p, sbv_p, sbk_s, sbv_s, conv_p, conv_s = [], [], [], [], [], []
    wk_p = [[] for _ in range(n_groups)]
    wv_p = [[] for _ in range(n_groups)]
    wk_s = [[] for _ in range(n_groups)]
    wv_s = [[] for _ in range(n_groups)]
    for l in range(DEPTH):
        p = tuple(a[l] for a in params)
        h_p, k, v, wk, wv, cr = layer_prompt(h_p, p, rel_bias)
        sbk_p.append(k)
        sbv_p.append(v)
        conv_p.append(cr)
        for g in range(n_groups):
            wk_p[g].append(wk[g])
            wv_p[g].append(wv[g])
        h_s, k, v, wk, wv, cr = layer_sample(h_s, p, rel_bias, cache_sb_k[l], cache_sb_v[l], page_table,
                                             tuple(c[l] for c in win_k_cache),
                                             tuple(c[l] for c in win_v_cache), state_conv[l])
        sbk_s.append(k)
        sbv_s.append(v)
        conv_s.append(cr)
        for g in range(n_groups):
            wk_s[g].append(wk[g])
            wv_s[g].append(wv[g])
    y_prompt = rmsnorm(h_p, norm_final_g)
    y_sample = rmsnorm(h_s, norm_final_g)
    sb_k_prompt = jnp.stack(sbk_p, axis=0)
    sb_v_prompt = jnp.stack(sbv_p, axis=0)
    sb_k_sample = jnp.stack(sbk_s, axis=0)
    sb_v_sample = jnp.stack(sbv_s, axis=0)
    win128_k_prompt = jnp.stack(wk_p[0], axis=0)
    win128_v_prompt = jnp.stack(wv_p[0], axis=0)
    win512_k_prompt = jnp.stack(wk_p[1], axis=0)
    win512_v_prompt = jnp.stack(wv_p[1], axis=0)
    win2048_k_prompt = jnp.stack(wk_p[2], axis=0)
    win2048_v_prompt = jnp.stack(wv_p[2], axis=0)
    win128_k_sample = jnp.stack(wk_s[0], axis=0)
    win128_v_sample = jnp.stack(wv_s[0], axis=0)
    win512_k_sample = jnp.stack(wk_s[1], axis=0)
    win512_v_sample = jnp.stack(wv_s[1], axis=0)
    win2048_k_sample = jnp.stack(wk_s[2], axis=0)
    win2048_v_sample = jnp.stack(wv_s[2], axis=0)
    conv_prompt = jnp.stack(conv_p, axis=0)
    conv_sample = jnp.stack(conv_s, axis=0)
    return (y_prompt, y_sample, sb_k_prompt, sb_v_prompt, sb_k_sample, sb_v_sample,
            win128_k_prompt, win128_v_prompt, win512_k_prompt, win512_v_prompt,
            win2048_k_prompt, win2048_v_prompt, win128_k_sample, win128_v_sample,
            win512_k_sample, win512_v_sample, win2048_k_sample, win2048_v_sample,
            conv_prompt, conv_sample)


_drawn_inputs = setup_inputs


def setup_inputs(seed=0):
    import zlib

    import numpy as np

    out = dict(_drawn_inputs(seed))
    spreads = {}
    factors = {'b_gate': 2.854,
     'b_sb': 8.0,
     'norm_mlp_g': 3.251,
     'rel_bias': 4.056,
     'norm_final_g': 2.791}
    for name, (base, spread) in spreads.items():
        noise = np.random.default_rng([zlib.crc32(name.encode()), seed]).standard_normal(out[name].shape)
        drawn = base * np.exp(spread * noise) if base else spread * noise
        out[name] = jnp.asarray(drawn.astype(out[name].dtype))
    for name, factor in factors.items():
        out[name] = (out[name] * factor).astype(out[name].dtype)
    return out
```

```python
import math
from contextlib import ExitStack

import numpy as np

import concourse.bass as bass
from concourse import mybir

F32 = mybir.dt.float32
F32R = mybir.dt.float32r
BF16 = mybir.dt.bfloat16
I32 = mybir.dt.int32
ALU = mybir.AluOpType
ACT = mybir.ActivationFunctionType
AX = mybir.AxisListType

P = 128
D = 1024
S = 512
NB = 8
TOK = S + NB
HALF = TOK // 2
KC = D // P
HD = 64
SBH = 8
DIL = ((128, 1), (512, 4), (2048, 16))
NG = 3
GH = 4
PAGES = 16
PAGE = 128
PAST = PAGES * PAGE
QB = S // P
SCALE = HD ** -0.5
EPS = 1e-6
MASK = -1e30
BUCKETS = 32
DFF = 4096
NU = 639

CB, CC, CH = 0, 512, 1024
SQ, SK, SV = 1536, 2048, 2560
DQ, DK, DV = 3072, 3840, 4608
GA = 5376


def bucket(dist):
    n = np.maximum(dist, 0)
    nf = np.maximum(n, 1).astype(np.float32)
    large = 16 + (np.log(nf / np.float32(16)) / np.float32(math.log(2048 / 16)) * np.float32(16)).astype(np.int32)
    return np.where(n < 16, n, np.minimum(large, BUCKETS - 1))


def bucket_tables():
    prompt = np.zeros((BUCKETS + 1, NG, NU + 1), np.float32)
    for g, (_, dil) in enumerate(DIL):
        for u in range(NU):
            dist = u - 127
            if dist >= 0 and dist % dil == 0 and dist // dil <= 128:
                prompt[bucket(np.array(dist)), g, u] = 1.0
            else:
                prompt[BUCKETS, g, u] = MASK
    sample = np.zeros((BUCKETS, NG, P), np.float32)
    for g, (_, dil) in enumerate(DIL):
        for i in range(P):
            sample[bucket(np.array((P - i) * dil)), g, i] = 1.0
    return prompt, sample


def slabs_before_mlp():
    out = []

    def proj(kind, col, tiles):
        for t in range(0, tiles, 2):
            out.append(dict(kind=kind, col=col + t * P, tile=t, nkc=KC, jobs=[(kind, 0, KC, "x")]))

    for kind, col, tiles in (("sq", SQ, 4), ("sk", SK, 4), ("sv", SV, 4), ("dq", DQ, 6), ("dk", DK, 6),
                             ("dv", DV, 6)):
        proj(kind, col, tiles)
    for t in (0, 2):
        for kind, col in (("cc", CC), ("ch", CH), ("cb", CB)):
            out.append(dict(kind=kind, col=col + t * P, tile=t, nkc=KC, jobs=[(kind, 0, KC, "x")]))
    for n in range(4):
        for b in range(3):
            out.append(dict(kind="gate", branch=b, col=GA + b * D + n * 256, tile=2 * n, nkc=KC,
                            jobs=[(f"g{b}", 0, KC, "x")]))
        out.append(dict(kind="ab", col=n * 256, tile=2 * n, nkc=8, jobs=[("ya", 0, 4, "conv"), ("yb", 4, 4, "sb")]))
        out.append(dict(kind="c", col=n * 256, tile=2 * n, nkc=2, jobs=[("yc", 0, 2, "dil")]))
    for n in range(4):
        out.append(dict(kind="out", col=n * 256, tile=2 * n, nkc=KC, jobs=[("out", 0, KC, "mixed")]))
    return out


SLABS = slabs_before_mlp()
UNITS = [(s, t) for s in range(len(SLABS)) for t in range(2)]
TICKS = []
for _u, (_s, _t) in enumerate(UNITS):
    for _j, _job in enumerate(SLABS[_s]["jobs"]):
        for _h in range(2):
            TICKS.append((_u, _job, _h, _j == len(SLABS[_s]["jobs"]) - 1 and _h == 1))
NT = len(TICKS)
LAST_TICK = {}
for _k, (_u, _job, _h, _l) in enumerate(TICKS):
    LAST_TICK[_u] = _k
ON_ACT = ("sq", "sk", "sv", "dq", "dk", "dv", "cc", "g0", "g1", "g2")
EVAC = []
_n = [0, 0]
for _u, _job, _h, _l in TICKS:
    _a = _job[0] in ON_ACT
    _n[_a] += 1
    EVAC.append((_a, _n[_a]))
GATE_TICK = next(k for k, t in enumerate(TICKS) if t[1][0] == "g0")
OUT_TICK = next(k for k, t in enumerate(TICKS) if t[1][0] == "out")
U_OF = {}
for _u, (_s, _t) in enumerate(UNITS):
    U_OF.setdefault((SLABS[_s]["kind"] + str(SLABS[_s].get("branch", "")), SLABS[_s]["tile"] + _t), _u)
NUNITS = len(UNITS)
WR = 3
GBANKS = 3
MR = 4
QUARTERS = 4
QT = DFF // P // QUARTERS
MSLABS = 2 * KC // 2


def at(kind, tile, half=1):
    return LAST_TICK[U_OF[kind, tile]] - (1 - half)


NKB = NB * PAGES // 2
SBI = QB * SBH
DLI = GH * QB


def make_plan():
    plan = [[] for _ in range(NT)]

    def add(tick, stage, n=0):
        plan[min(tick, NT - 1)].append((stage, n))

    end = GATE_TICK - 1
    add(4, "tables")
    t0 = at("sq", 3) + 2
    add(t0, "q_rows")
    for b in range(NB):
        add(min(t0 + 1 + 8 * b, end), "q_spread", b)
    kt = [min(t0 + 2 + n, end) for n in range(NKB)]
    for i in range(QB + 1):
        add(at("sk", 3) + 1 + i, "sk_rows", i)
        add(at("sv", 3) + 1 + i, "sv_rows", i)
    s0 = at("sv", 3)
    late = []
    add(t0 - 1, "k_load", 0)
    add(t0, "k_load", 1)
    for n in range(NKB):
        add(kt[n], "k_scores", n)
        if n + 2 < NKB:
            add(kt[n], "k_load", n + 2)
    for b in range(NB):
        t = min(kt[8 * b + 7] + 1, end)
        add(t, "d_softplus", b)
        add(min(t + 1, end), "d_suffix", b)
        add(min(t + 2, end), "d_weights", b)
        for n in range(8):
            if 8 * b + n < 2:
                add(t, "v_load", 8 * b + n)
            late.append((min(t + 3 + n, end), "v_sum", 8 * b + n))
            if 8 * b + n + 2 < NKB:
                late.append((min(t + 3 + n, end), "v_load", 8 * b + n + 2))
    for n in range(SBI):
        t = s0 + n
        add(t, "p_scores", n)
        add(t + 1, "p_weights", n)
        add(t + 2, "p_turn", n)
        add(t + 3, "p_sum", n)
        if n % SBH == SBH - 1:
            add(t + 4, "p_out", n // SBH)
    p1 = s0 + SBI + 4
    add(p1, "phase", 1)
    for i in range(QB + 1):
        for part in range(2):
            add(at("dk", 5) + 1 + i, "dk_rows", 2 * i + part)
    for g in range(NG):
        for r in range(3):
            add(at("dv", 2 * g + 1) + 1 + r, "dv_rows", 3 * g + r)
    d0 = max(p1, at("dv", 5) + 4) + 1
    for j in range(GH):
        for i in range(QB):
            n = QB * j + i
            t = d0 + n
            if i == 0:
                add(d0 - 1 if j < 2 else d0 + QB * (j - 1), "bias_load", j)
            add(t, "l_scores", n)
            add(t + 1, "l_weights", n)
            add(t + 2, "l_sum", n)
        if j % 2:
            add(t + 3, "l_out", j // 2)
    add(p1 + 1, "conv_state")
    add(at("cb", 3), "conv_rows")
    for t, stage, n in late:
        add(t, stage, n)
    add(end, "d_out")
    add(end, "phase", 2)
    add(end, "s_rows")
    for g in range(NG):
        add(end, "s_load", g)
    for n in range(4 * NG):
        add(end, "s_scores", n)
    add(end, "s_self")
    for g in range(NG):
        add(end, "s_turn", g)
    add(end, "s_soft")
    add(end, "s_back")
    add(end, "s_sum")
    add(end, "phase", 3)
    add(end, "branch_split", 0)
    add(OUT_TICK - 1, "phase", 4)
    add(OUT_TICK - 1, "x_again")
    for t in range(KC):
        add(OUT_TICK - 1 + 2 * t, "x_turn", t)
    return plan


PLAN = make_plan()

USES = {"S0": [], "S1": [], "TR": [], "OU": []}
SPOT = {}


def use(bank, *key):
    SPOT[key] = (bank, len(USES[bank]))
    USES[bank].append(key)


use("TR", "x_norm", KC)
for _c in range(KC):
    use("TR" if _c % 2 else "OU", "x_norm", _c)
_s_count = [0]


def _score_use(*key):
    use(f"S{_s_count[0] % 2}", *key)
    _s_count[0] += 1


for _k in range(NT):
    for _stage, _n in PLAN[_k]:
        if _stage == "tables":
            for _g in range(NG):
                _score_use("table", _g, 0)
                _score_use("table", _g, 1)
            _score_use("table_s")
        elif _stage in ("q_spread", "d_suffix", "p_scores", "s_scores"):
            _score_use(_stage, _n)
        elif _stage == "l_scores":
            for _g in range(NG):
                _score_use(_stage, _n, _g)
        elif _stage in ("q_rows", "sk_rows", "sv_rows", "p_turn", "p_out", "dk_rows", "l_out",
                        "conv_state", "conv_rows", "s_turn", "s_back"):
            use("TR", _stage, _n)
        elif _stage == "x_turn":
            use("TR", _stage, _n, "prompt")
            use("OU", _stage, _n, "sample")
        elif _stage == "dv_rows":
            use("TR", _stage, _n)
        elif _stage == "s_rows":
            for _r in range(4):
                use("TR", _stage, _r)
        elif _stage == "l_sum":
            for _g in range(NG):
                use("TR", "l_turn", _n, _g)
            if _n % QB == 0:
                use("OU", "l_sum", _n // QB)
        elif _stage == "p_sum" and _n % SBH == 0:
            use("OU", "p_sum", _n // SBH)
        elif _stage == "s_sum":
            use("OU", "s_sum")


def decoder_step(nc, x, o, w):
    ctx = ExitStack()
    with ctx:
        def sem(name):
            return ctx.enter_context(nc.semaphore(name))

        def psum(name, dt=F32):
            return ctx.enter_context(nc.psum_tensor(name, [P, 512], dt))

        base = 16512

        def place(name, shape, col, dt=F32):
            return nc.alloc_sbuf_tensor_at(name, shape, dt, offset=base + 4 * col)

        xh = place("xh", [P, KC, TOK], 0, F32R)
        xl = place("xl", [P, KC, TOK], 4160, F32R)
        wraw = place("wraw", [P, WR, KC, 256], 8320)
        whi = place("whi", [P, 2, KC, P], 14464, F32R)
        wlo = place("wlo", [P, 2, KC, P], 16512, F32R)
        ident = place("ident", [P, P], 18560)
        identb = place("identb", [P, P], 18688, BF16)
        maskb = place("maskb", [P, P], 18752, BF16)
        tri = place("tri", [P, P], 18816)
        ones = place("ones", [P, P], 18944)
        gmix = place("gmix", [P, KC], 19072)
        gmlp = place("gmlp", [P, KC], 19080)
        bgate = place("bgate", [P, 3, KC], 19088)
        bsb = place("bsb", [P, SBH], 19112)
        convw = place("convw", [P, 3, 4], 19120)
        selfbias = place("selfbias", [NB, 12], 19136)
        stepbias = place("stepbias", [P, 12], 19152)
        ss = place("ss", [P, 8], 19168)
        rms = place("rms", [P, 8], 19176)
        rstd = place("rstd", [P, 8], 19184)
        pages = place("pages", [1, NB * PAGES], 19192, I32)
        stat = place("stat", [P, 2, 8], 19320)
        smax = place("smax", [NB, 4], 19336)
        ssum = place("ssum", [NB, 4], 19344)
        sself = place("sself", [NB, 12], 19352)
        q_row = place("q_row", [NB, 512], 19368)
        relb = place("relb", [BUCKETS + 1, 12], 19880)
        stT = place("stT", [P, 4, NB, 2], 19896)
        utail = place("utail", [P, 4, 10], 19960)
        R = 20608
        xrow = place("xrow", [P, QB, D], R)
        xsrow = place("xsrow", [NB, D], R + 4096)
        nrow = place("nrow", [P, QB, D], R + 6208)
        nsrow = place("nsrow", [NB, D], R + 10304)
        xjunk = place("xjunk", [P, D], R + 12448)
        xn = place("xn", [P, 2, TOK], R + 15520)
        hot = place("hot", [BUCKETS + 1, NG, NU + 1], R + 19104)
        btab = place("btab", [GH, NG, NU + 1], R + 21024)
        hots = place("hots", [BUCKETS, NG, P], R + 24224)
        sqT = place("sqT", [P, 4, TOK], R)
        skT = place("skT", [P, 4, TOK], R + 2080)
        sv_tok = place("sv_tok", [P, QB, 512], R + 4160)
        svT = place("svT", [P, 4, TOK], R + 9328)
        pz = place("pz", [P, 2, 512], R + 15520)
        psp = place("psp", [P, 2, 512], R + 16544)
        pw = place("pw", [P, 2, 512], R + 17568)
        pT = place("pT", [P, 512], R + 18592)
        dqT = place("dqT", [P, 6, TOK], R + 6208)
        dkT = place("dkT", [P, 6, TOK], R + 9328)
        dv_tok = place("dv_tok", [P, QB, 768], R + 12448)
        bias = place("bias", [P, 2, 1280], R)
        lg = place("lg", [P, 2, 1280], R + 15520)
        lT = place("lT", [P, 2, 512], R + 18080)
        convu = place("convu", [P, 2, 2 + TOK], R + 2560)
        convy = place("convy", [P, 4, TOK], R + 3608)
        st_row = place("st_row", [2 * NB, 512], R + 5688)
        kpg = place("kpg", [P, 4, 512], R + 19104)
        vpg = place("vpg", [P, 4, 512], R + 21152)
        prod = place("prod", [P, 2, 512], R + 23200)
        qs = place("qs", [P, 2, 512], R + 24224)
        dw = place("dw", [P, 2, PAGES, SBH], R + 25248)
        dz = place("dz", [P, PAGES, SBH], R + 25504)
        de = place("de", [P, PAGES, SBH], R + 25632)
        dsp = place("dsp", [P, PAGES, SBH], R + 25760)
        dr = place("dr", [P, 2, PAGES, SBH], R + 25888)
        zs = place("zs", [P, 2, PAGES, SBH], R + 26272)
        vd_row = place("vd_row", [NB, 768], R + 26528)
        krow = place("krow", [P, 512], R + 27296)
        o_sbT = place("o_sbT", [P, 4, TOK], R + 27808)
        dvT = place("dvT", [P, 2, 2, TOK], R + 29888)
        o_dT = place("o_dT", [P, 2, TOK], R + 30928)
        o_tok = place("o_tok", [P, 512], R + 31968)
        sK = [place(f"sK{g}", [P, NB, 256], R + 12448 + 2048 * g) for g in range(NG)]
        sV = [place(f"sV{g}", [P, NB, 256], R + 18592 + 2048 * g) for g in range(NG)]
        sprod = place("sprod", [P, 2, 256], R + 24736)
        sz = place("sz", [P, NG, NB, GH], R + 25248)
        srprod = place("srprod", [NB, 768], R + 25344)
        spT = place("spT", [P, NG, GH, NB], R + 26112)
        spself = place("spself", [NB, NG, GH, NB], R + 26208)
        slog = place("slog", [NB, GH, NG, P + 1], R)
        qd_row = place("qd_row", [NB, 768], R + 1552)
        kd_row = place("kd_row", [NB, 768], R + 2320)
        tg = place("tg", [P, 3, 2, TOK], R)
        binh = place("binh", [P, 10, TOK], R + 6208, F32R)
        binl = place("binl", [P, 10, TOK], R + 11408, F32R)
        mixh = place("mixh", [P, KC, TOK], R + 16608, F32R)
        mixl = place("mixl", [P, KC, TOK], R + 20768, F32R)
        macc = place("macc", [P, 2, TOK], R + 24928)
        mtmp = place("mtmp", [P, 2, HALF], R + 25968)
        xarow = place("xarow", [P, QB, D], R + 6208)
        xasrow = place("xasrow", [NB, D], R + 10304)
        hT = place("hT", [P, KC, TOK], R + 11408)
        mraw = place("mraw", [P, MR, KC, 256], R)
        hidh = place("hidh", [P, QT, TOK], R + 16608, F32R)
        hidl = place("hidl", [P, QT, TOK], R + 20768, F32R)
        hacc = place("hacc", [P, TOK], R + 26528)
        h2 = place("h2", [P, TOK], R + 27296 + 512)
        rstdb = place("rstdb", [P, TOK], R + 28848)
        mt = place("mt", [P, 2, HALF], R + 29368)
        msq = place("msq", [P, 2, HALF], R + 29888)
        hn = place("hn", [P, 2, TOK], R + 30408)
        gfin = place("gfin", [P, D], R + 8192)
        yrow = place("yrow", [P, 2, D], R + 9216)
        yjunk = place("yjunk", [P, D], R + 15568)

        G = [psum(f"G{i}") for i in range(GBANKS)]
        bank = {n: psum(n) for n in ("S0", "S1", "TR", "OU")}
        DEC = psum("DEC")
        MB = [*G, bank["S0"]]
        dec_sum = DEC[:, 0:NB * SBH].rearrange("p (b t e) -> p b t e", b=NB, e=2)

        x_in = sem("x_in")
        const_in = [sem(f"const_in{i}") for i in range(13)]
        hot_in, hots_in, pages_in, table_out = (sem(n) for n in ("hot_in", "hots_in", "pages_in", "table_out"))
        w_in_slot = [sem(f"w_in_slot{i}") for i in range(WR)]
        m_in_slot = [sem(f"m_in_slot{i}") for i in range(MR)]
        w_hi, w_lo, made = sem("w_hi"), sem("w_lo"), sem("made")
        act_took, dve_took = sem("act_took"), sem("dve_took")
        written = {n: sem(f"written_{n}") for n in bank}
        read = {n: sem(f"read_{n}") for n in bank}
        act_done, dve_done, pool_done = sem("act_done"), sem("dve_done"), sem("pool_done")
        consts_made = sem("consts_made")
        x_scaled, x_normed, xh_made, xl_made = (sem(n) for n in ("x_scaled", "x_normed", "xh_made", "xl_made"))
        phase_reached = sem("phase_reached")
        k_in = [sem(f"k_in{i}") for i in range(2)]
        v_in = [sem(f"v_in{i}") for i in range(2)]
        k_used, v_used, z_made = sem("k_used"), sem("v_used"), sem("z_made")
        bgate_made = sem("bgate_made")
        d_made, d_abs, d_ln, d_wmade = sem("d_made"), sem("d_abs"), sem("d_ln"), sem("d_wmade")
        d_spmade, d_cmade, dec_made = sem("d_spmade"), sem("d_cmade"), sem("dec_made")
        p_zmade, p_lnmade, p_wmade, p_amade, p_Tmade = (sem(n) for n in ("p_zmade", "p_lnmade", "p_wmade", "p_amade", "p_Tmade"))
        o_made = sem("o_made")
        bias_in_slot = [sem(f"bias_in_slot{i}") for i in range(2)]
        krow_out, v_out, vdrow_out, row_out = (sem(n) for n in ("krow_out", "v_out", "vdrow_out", "row_out"))
        l_made, l_pmade, l_Tmade = sem("l_made"), sem("l_pmade"), sem("l_Tmade")
        st_in, st_made = sem("st_in"), sem("st_made")
        conv_made = sem("conv_made")
        sK_in = [sem(f"sK_in{g}") for g in range(NG)]
        sV_in = [sem(f"sV_in{g}") for g in range(NG)]
        s_rowsmade, s_zmade, s_Tmade, s_pmade, s_backmade = (sem(n) for n in ("s_rowsmade", "s_zmade", "s_Tmade", "s_pmade", "s_backmade"))
        bin_hi, bin_lo = sem("bin_hi"), sem("bin_lo")
        mix_ready, mix_hi, mix_lo = sem("mix_ready"), sem("mix_hi"), sem("mix_lo")
        xa_in, hT_made, h_ready, h2_made, hacc_made, hn_made = (sem(n) for n in ("xa_in", "hT_made", "h_ready", "h2_made", "hacc_made", "hn_made"))
        hn_hi, hn_lo = sem("hn_hi"), sem("hn_lo")
        var_made, var_read, sd_made, rstdb_made = (sem(n) for n in ("var_made", "var_read", "sd_made", "rstdb_made"))
        m_made, m_took, m_relu, m_sq, hid_hi, hid_lo = (sem(n) for n in ("m_made", "m_took", "m_relu", "m_sq", "hid_hi", "hid_lo"))
        gfin_in, y_T, y_sum, y_sd, y_rstd, y_made = (sem(n) for n in ("gfin_in", "y_T", "y_sum", "y_sd", "y_rstd", "y_made"))
        y_out = [sem("y_out0"), sem("y_out1")]
        win_out = sem("win_out")

        slab_load = []
        filled = [0] * WR
        for s_, slab_ in enumerate(SLABS):
            filled[s_ % WR] += 32 if slab_["kind"] == "ab" else 16
            slab_load.append((s_ % WR, filled[s_ % WR]))

        def half(h):
            return slice(h * HALF, (h + 1) * HALF)

        def took(k):
            on_act, n = EVAC[k]
            return (act_took if on_act else dve_took), n

        def open_bank(pe, *key):
            name, n = SPOT[key]
            if n:
                pe.wait_ge(read[name], n)
            return bank[name]

        def await_bank(eng, *key):
            name, n = SPOT[key]
            eng.wait_ge(written[name], n + 1)
            return bank[name]

        def await_taken(eng, *key):
            name, n = SPOT[key]
            eng.wait_ge(read[name], n + 1)

        def of(sems, *key):
            return sems[SPOT[key][0]]

        def n_keys(i):
            n = P * (i + 1)
            n0 = min(2 * P, n)
            return n, n0, n0 + 2 * n

        def head(h):
            return h // 2, slice(HD * (h % 2), HD * (h % 2) + HD)

        krow_before, stores = {}, 0
        v_stores = QB
        for k_ in range(NT):
            for stage_, n_ in PLAN[k_]:
                if stage_ in ("sk_rows", "dk_rows", "conv_rows"):
                    krow_before[stage_, n_] = stores
                    if stage_ == "dk_rows":
                        gs = (0, 1) if n_ % 2 == 0 else (2,)
                        stores += sum(n_ // 2 == QB or P * (n_ // 2) >= S - min(DIL[g][0], S) for g in gs)
                    else:
                        stores += 2 if stage_ == "conv_rows" else 1
        v_stores += sum(1 for g in range(NG) for i in range(QB) if P * i >= S - min(DIL[g][0], S))

        source = {"x": (xh, xl, 0), "conv": (binh, binl, 0), "sb": (binh, binl, 4), "dil": (binh, binl, 8),
                  "mixed": (mixh, mixl, 0)}

        block = ctx.enter_context(nc.Block())

        @block.sync
        def _(sp):
            def load_slab(s):
                slab = SLABS[s]
                slot = s % WR
                if s >= WR:
                    sp.wait_ge(w_lo, 2 * (s - WR) + 2)
                cols = slice(slab["col"], slab["col"] + 256)
                if slab["kind"] == "ab":
                    parts = ((x["w_branch_conv"], 0, 4), (x["w_branch_sb"], 4, 4))
                elif slab["kind"] == "c":
                    parts = ((x["w_branch_dil"], 0, 2),)
                else:
                    parts = ((x["w_out"] if slab["kind"] == "out" else x["w_in"], 0, KC),)
                for src, k0, n in parts:
                    sp.dma_start(wraw[:, slot, k0:k0 + n, :],
                                 src[0].rearrange("(k p) n -> p k n", p=P)[:, :, cols]).then_inc(w_in_slot[slot], 16)

            sp.dma_start(xrow[:], x["x_prompt"][0].rearrange("(i p) d -> p i d", p=P)).then_inc(x_in, 16)
            sp.dma_start(xsrow[:], x["x_sample"].rearrange("b t d -> (b t) d")).then_inc(x_in, 16)
            load_slab(0)
            load_slab(1)
            with nc.allow_non_contiguous_dma(reason="small vectors, one element per partition"):
                smalls = [(gmix[:], x["norm_mix_g"][0].rearrange("(k p) -> p k", p=P)),
                          (gmlp[:], x["norm_mlp_g"][0].rearrange("(k p) -> p k", p=P)),
                          (bgate[:, 0, :], x["b_gate"][0, 0].rearrange("(k p) -> p k", p=P)),
                          (bgate[:, 1, :], x["b_gate"][0, 1].rearrange("(k p) -> p k", p=P)),
                          (bgate[:, 2, :], x["b_gate"][0, 2].rearrange("(k p) -> p k", p=P)),
                          (convw[:, 0, :], x["conv_w"][0, 0].rearrange("(k p) -> p k", p=P)),
                          (convw[:, 1, :], x["conv_w"][0, 1].rearrange("(k p) -> p k", p=P)),
                          (convw[:, 2, :], x["conv_w"][0, 2].rearrange("(k p) -> p k", p=P)),
                          (bsb[:], x["b_sb"][0].partition_broadcast(P)),
                          (selfbias[:], x["rel_bias"][0].partition_broadcast(NB)),
                          (relb[0:BUCKETS, :], x["rel_bias"])]
                for n, (dst, src) in enumerate(smalls):
                    sp.dma_start(dst, src).then_inc(const_in[n], 16)
            sp.dma_start(pages[:], x["page_table"].rearrange("(a b) n -> a (b n)", a=1)).then_inc(pages_in, 16)
            sp.dma_start(hot[:], x["hot"]).then_inc(hot_in, 16)
            sp.dma_start(hots[:], x["hots"]).then_inc(hots_in, 16)
            sp.wait_ge(pages_in, 16)

            def page_load(dst, pool, n, landed):
                for p in range(2):
                    b_page = 2 * n + p
                    page = sp.value_load(pages[0:1, b_page:b_page + 1], min_val=0, max_val=pool.shape[1] - 1)
                    sp.dma_start(dst[:, 2 * (n % 2) + p, :],
                                 pool[0, bass.ds(page, 1)].rearrange("a t h d -> (a t) (h d)")).then_inc(landed, 16)

            def k_load(n):
                if n == 0:
                    sp.wait_ge(table_out, 16)
                if n >= 2:
                    sp.wait_ge(k_used, n - 1)
                page_load(kpg, x["cache_sb_k"], n, k_in[n % 2])

            def v_load(n):
                if n == 0:
                    sp.wait_ge(table_out, 16)
                if n >= 2:
                    sp.wait_ge(v_used, n - 1)
                page_load(vpg, x["cache_sb_v"], n, v_in[n % 2])

            def tables(_):
                for g in range(NG):
                    await_taken(sp, "table", g, 0)
                    await_taken(sp, "table", g, 1)
                await_taken(sp, "table_s")
                sp.dma_start(w["btab"], btab[:]).then_inc(table_out, 16)

            def bias_load(j):
                if j == 0:
                    sp.wait_ge(table_out, 16)
                if j >= 2:
                    sp.wait_ge(l_made, QB * (j - 1))
                tab = w["btab"]
                for g, (col, n) in enumerate(((0, 256), (256, 512), (768, 512))):
                    src = bass.AP(tensor=tab.tensor, offset=(j * NG + g) * (NU + 1), ap=[[1, P], [1, n]])
                    sp.dma_start(bias[:, j % 2, col:col + n], src).then_inc(bias_in_slot[j % 2], 16)

            def sk_rows(i):
                await_taken(sp, "sk_rows", i)
                if i < QB:
                    sp.dma_start(o["sb_k_prompt"][0, 0, P * i:P * i + P].rearrange("t h d -> t (h d)"), krow[:]).then_inc(krow_out, 16)
                else:
                    sp.dma_start(o["sb_k_sample"][0, :, 0].rearrange("b h d -> b (h d)"), krow[0:NB, :]).then_inc(krow_out, 16)

            def sv_rows(i):
                await_taken(sp, "sv_rows", i)
                if i < QB:
                    sp.dma_start(o["sb_v_prompt"][0, 0, P * i:P * i + P].rearrange("t h d -> t (h d)"), sv_tok[:, i, :]).then_inc(v_out, 16)
                else:
                    sp.dma_start(o["sb_v_sample"][0, :, 0].rearrange("b h d -> b (h d)"), vd_row[:, 0:512]).then_inc(vdrow_out, 16)

            def dk_rows(n):
                i, part = n // 2, n % 2
                await_taken(sp, "dk_rows", n)
                for g in ((0, 1) if part == 0 else (2,)):
                    src = krow[:, 256 * (g % 2):256 * (g % 2) + 256]
                    name = f"win{DIL[g][0]}_k"
                    if i < QB:
                        rows = o[name + "_prompt"]
                        first = S - rows.shape[2]
                        if P * i < first:
                            continue
                        sp.dma_start(rows[0, 0, P * i - first:P * i - first + P].rearrange("t h d -> t (h d)"), src).then_inc(krow_out, 16)
                    else:
                        rows = o[name + "_sample"]
                        sp.dma_start(rows[0, :, rows.shape[2] - 1].rearrange("b h d -> b (h d)"), src[0:NB]).then_inc(krow_out, 16)

            def dv_rows(n):
                g, r = n // 3, n % 3
                name = f"win{DIL[g][0]}_v"
                await_taken(sp, "dv_rows", n)
                if r < 2:
                    rows = o[name + "_prompt"]
                    first = S - rows.shape[2]
                    for i in (2 * r, 2 * r + 1):
                        if P * i >= first:
                            sp.dma_start(rows[0, 0, P * i - first:P * i - first + P].rearrange("t h d -> t (h d)"),
                                         dv_tok[:, i, 256 * g:256 * g + 256]).then_inc(v_out, 16)
                else:
                    rows = o[name + "_sample"]
                    sp.dma_start(rows[0, :, rows.shape[2] - 1].rearrange("b h d -> b (h d)"),
                                 vd_row[:, 256 * g:256 * g + 256]).then_inc(row_out, 16)

            def phase(n):
                sp.wait_ge(phase_reached, 4 * n)
                if n == 1:
                    sp.dma_start(st_row[:], x["state_conv"][0].rearrange("b k c -> (b k) c")).then_inc(st_in, 16)

            def conv_rows(_):
                await_taken(sp, "conv_rows", 0)
                sp.dma_start(o["conv_prompt"][0, 0], krow[0:2, :]).then_inc(krow_out, 16)
                sp.dma_start(o["conv_sample"][0, :, 1], krow[2:10, :]).then_inc(krow_out, 16)
                sp.dma_start(o["conv_sample"][0, :, 0], x["state_conv"][0, :, 1]).then_inc(row_out, 16)

            def s_load(g):
                window, dil = DIL[g]
                for dst, kind, landed in ((sK[g], "k", sK_in[g]), (sV[g], "v", sV_in[g])):
                    cache = x[f"cache_win{window}_{kind}"][0].rearrange("b (i r) h d -> i b r (h d)", r=dil)
                    sp.dma_start(dst[:], cache[:, :, 0]).then_inc(landed, 16)

            def x_again(_):
                sp.dma_start(xarow[:], x["x_prompt"][0].rearrange("(i p) d -> p i d", p=P)).then_inc(xa_in, 16)
                sp.dma_start(xasrow[:], x["x_sample"].rearrange("b t d -> (b t) d")).then_inc(xa_in, 16)

            stages = dict(k_load=k_load, v_load=v_load, tables=tables, bias_load=bias_load, sk_rows=sk_rows,
                          sv_rows=sv_rows, dk_rows=dk_rows, dv_rows=dv_rows, phase=phase, conv_rows=conv_rows,
                          s_load=s_load, x_again=x_again)
            for k, (u, job, h, last) in enumerate(TICKS):
                s, t = UNITS[u]
                if t == 0 and k == (LAST_TICK[u - 1] + 1 if u else 0) and s + 2 < len(SLABS):
                    load_slab(s + 2)
                for stage, n in PLAN[k]:
                    if stage in stages:
                        stages[stage](n)

            up = x["w_mlp_up"][0].rearrange("(k p) n -> p k n", p=P)
            down = x["w_mlp_down"][0].rearrange("(q k p) n -> q p k n", p=P, k=QT)
            win_copies = []
            for window, _ in DIL:
                for kind in "kv":
                    win_copies.append((o[f"win{window}_{kind}_sample"][0], x[f"cache_win{window}_{kind}"][0], window))

            def flat16(rows):
                return rows.rearrange("b t h d -> (b t h d)").rearrange("(a n) -> a n", a=16)

            sp.wait_ge(phase_reached, 4 * 5)
            with sp.Fori(0, QUARTERS) as q:
                for m in range(MSLABS):
                    sp.wait_ge(w_lo, NUNITS + q * (2 * MSLABS) + 2 * (m - MR) + 2)
                    if m < MR:
                        src = up[:, :, bass.ds(q * (QT * P) + 256 * m, 256)]
                    else:
                        src = down[bass.ds(q, 1), :, :, 256 * (m - MR):256 * (m - MR) + 256].rearrange("a p k n -> (a p) k n")
                    sp.dma_start(mraw[:, m % MR], src).then_inc(m_in_slot[m % MR], 16)
                for dst, src, window in win_copies:
                    for b in range(NB // QUARTERS):
                        sample = bass.ds(q * (NB // QUARTERS) + b, 1)
                        sp.dma_start(flat16(dst[sample, 0:window - 1]), flat16(src[sample, 1:window])).then_inc(win_out, 16)
            sp.dma_start(gfin[:], x["norm_final_g"].partition_broadcast(P)).then_inc(gfin_in, 16)
            for i in range(QB + 1):
                sp.wait_ge(y_made, 2 * (i + 1))
                if i < QB:
                    sp.dma_start(o["y_prompt"][0, P * i:P * i + P], yrow[:, i % 2, :]).then_inc(y_out[i % 2], 16)
                else:
                    sp.dma_start(o["y_sample"].rearrange("b t d -> (b t) d"), yrow[0:NB, i % 2, :]).then_inc(y_out[i % 2], 16)
            sp.wait_ge(y_out[0], 16 * 3)
            sp.wait_ge(y_out[1], 16 * 2)
            sp.wait_ge(win_out, 16 * 6 * NB)
            sp.wait_ge(row_out, 16 * 4)
            sp.wait_ge(vdrow_out, 16)
            sp.wait_ge(v_out, 16 * v_stores)
            sp.wait_ge(krow_out, 16 * stores)

        @block.gpsimd
        def _(pool):
            nc.gpsimd.memset(ident[:], 0.0).then_inc(pool_done, 1)
            nc.gpsimd.memset(identb[:], 0.0).then_inc(pool_done, 1)
            nc.gpsimd.memset(maskb[:], 0.0).then_inc(pool_done, 1)
            nc.gpsimd.memset(tri[:], 1.0).then_inc(pool_done, 1)
            nc.gpsimd.memset(ones[:], 1.0).then_inc(consts_made, 1)
            pool.wait_ge(pool_done, 4)
            for m in (ident, identb):
                nc.gpsimd.affine_select(out=m[:], in_=m[:], compare_op=ALU.not_equal, fill=1.0, base=0,
                                        pattern=[[-1, P]], channel_multiplier=1).then_inc(consts_made, 1)
            nc.gpsimd.affine_select(out=maskb[:], in_=maskb[:], compare_op=ALU.is_gt, fill=MASK, base=0,
                                    pattern=[[-1, P]], channel_multiplier=1).then_inc(consts_made, 1)
            nc.gpsimd.affine_select(out=tri[:], in_=tri[:], compare_op=ALU.is_ge, fill=0.0, base=0,
                                    pattern=[[-1, P]], channel_multiplier=1).then_inc(consts_made, 1)

            def split_lo(u):
                s, t = UNITS[u]
                n = SLABS[s]["nkc"]
                pool.wait_ge(w_hi, u + 1)
                nc.gpsimd.tensor_tensor(wlo[:, u % 2, 0:n, :], wraw[:, s % WR, 0:n, P * t:P * t + P],
                                        whi[:, u % 2, 0:n, :].bitcast(F32), ALU.subtract).then_inc(w_lo, 1)

            split_lo(0)
            split_lo(1)
            for k, (u, job, h, last) in enumerate(TICKS):
                if last and u + 2 < NUNITS:
                    split_lo(u + 2)
                for stage, n in PLAN[k]:
                    if stage == "phase":
                        if n == 1:
                            pool.wait_ge(v_out, 16 * QB)
                        if n == 2:
                            pool.wait_ge(v_out, 16 * v_stores)
                            pool.wait_ge(krow_out, 16 * stores)
                            pool.wait_ge(row_out, 16 * 4)
                        nc.gpsimd.drain().then_inc(phase_reached, 1)
                        pool.wait_ge(phase_reached, 4 * n)
            nc.gpsimd.drain().then_inc(phase_reached, 1)
            with pool.Fori(0, QUARTERS) as q:
                for u in range(2 * MSLABS):
                    pool.wait_ge(w_hi, NUNITS + q * (2 * MSLABS) + u + 1)
                    nc.gpsimd.tensor_tensor(wlo[:, u % 2], mraw[:, (u // 2) % MR, :, P * (u % 2):P * (u % 2) + P],
                                            whi[:, u % 2].bitcast(F32), ALU.subtract).then_inc(w_lo, 1)

        @block.scalar
        def _(act):
            done = [0]

            def link(ins):
                done[0] += 1
                ins.then_inc(act_done, 1)
                act.wait_ge(act_done, done[0])

            def copy(out, in_, **kw):
                return nc.scalar.activation(out, in_, ACT.Copy, **kw)

            for n in (2, 3, 4, 8):
                act.wait_ge(const_in[n], 16)
            act.wait_ge(consts_made, 6)
            act.wait_ge(x_in, 32)
            for i in range(QB):
                link(nc.scalar.activation(xjunk[:], xrow[:, i, :], ACT.Square, accum_out=ss[:, i:i + 1]))
            link(nc.scalar.activation(xjunk[0:NB, :], xsrow[:], ACT.Square, accum_out=ss[0:NB, QB:QB + 1]))
            act.wait_ge(dve_done, 2)
            link(nc.scalar.activation(rms[:, 0:QB], rms[:, 0:QB], ACT.Sqrt))
            link(nc.scalar.activation(rms[0:NB, QB:QB + 1], rms[0:NB, QB:QB + 1], ACT.Sqrt))

            def split_hi(u):
                s, t = UNITS[u]
                n = SLABS[s]["nkc"]
                if t == 0:
                    act.wait_ge(w_in_slot[slab_load[s][0]], slab_load[s][1])
                if u >= 2:
                    act.wait_ge(made, LAST_TICK[u - 2] + 1)
                copy(whi[:, u % 2, 0:n, :], wraw[:, s % WR, 0:n, P * t:P * t + P]).then_inc(w_hi, 1)

            split_hi(0)
            await_taken(act, "x_norm", KC)
            copy(xh[:, :, S:TOK], xjunk[:, 0:KC * NB].rearrange("p (k b) -> p k b", k=KC)).then_inc(xh_made, 1)
            for c in range(KC):
                await_taken(act, "x_norm", c)
                copy(xh[:, c, 0:S], xn[:, c % 2, 0:S]).then_inc(xh_made, 1)
                if c == 1:
                    split_hi(1)

            plain = dict(sq=sqT, sk=skT, sv=svT, dq=dqT, dk=dkT)

            def take(k):
                u, job, h, last = TICKS[k]
                s, t = UNITS[u]
                kind, tile = job[0], SLABS[s]["tile"] + t
                act.wait_ge(made, k + 1)
                src = G[k % GBANKS][:, 0:HALF]
                if kind in plain:
                    if kind == "dk" and tile == 0 and h == 0:
                        await_bank(act, "sv_rows", QB)
                    copy(plain[kind][:, tile, half(h)], src).then_inc(act_took, 1)
                elif kind == "dv":
                    g = tile // 2
                    if g == 2 and tile % 2 == 0 and h == 0:
                        await_bank(act, "dv_rows", 3 * (g - 2) + 2)
                    copy(dvT[:, g % 2, tile % 2, half(h)], src).then_inc(act_took, 1)
                elif kind == "cc":
                    if tile >= 2:
                        act.wait_ge(conv_made, tile - 1)
                    copy(convu[:, tile % 2, 2 + h * HALF:2 + h * HALF + HALF], src).then_inc(act_took, 1)
                else:
                    g = int(kind[1])
                    if k == GATE_TICK:
                        act.wait_ge(bgate_made, 1)
                    if tile >= 2 and g == 0 and t == 0 and h == 0:
                        act.wait_ge(mix_ready, 2 * tile)
                    nc.scalar.activation(tg[:, g, t, half(h)], src, ACT.Tanh, scale=0.5,
                                         bias=bgate[:, g, tile:tile + 1]).then_inc(act_took, 1)

            def tables(_):
                for g in range(NG):
                    for part, (c, n) in enumerate(((0, 512), (512, NU + 1 - 512))):
                        src = await_bank(act, "table", g, part)
                        copy(btab[:, g, c:c + n], src[0:GH, 0:n]).then_inc(of(read, "table", g, part), 1)
                copy(stepbias[:], await_bank(act, "table_s")[:, 0:12]).then_inc(of(read, "table_s"), 1)

            def q_rows(_):
                copy(q_row[:], await_bank(act, "q_rows", 0)[0:NB, :]).then_inc(read["TR"], 1)

            def q_spread(b):
                if b >= 2:
                    act.wait_ge(k_used, PAGES // 2 * (b - 1))
                copy(qs[:, b % 2, :], await_bank(act, "q_spread", b)[:, :]).then_inc(of(read, "q_spread", b), 1)

            def to_krow(stage, n, rows, cols):
                if krow_before[stage, n]:
                    act.wait_ge(krow_out, 16 * krow_before[stage, n])
                src = await_bank(act, stage, n)
                copy(krow[0:rows, 0:cols], src[0:rows, 0:cols]).then_inc(read["TR"], 1)

            def sk_rows(i):
                to_krow("sk_rows", i, P if i < QB else NB, 512)

            def dk_rows(n):
                to_krow("dk_rows", n, P if n < 2 * QB else NB, 512 if n % 2 == 0 else 256)

            def conv_rows(_):
                to_krow("conv_rows", 0, 2 + NB, 512)

            def sv_rows(i):
                src = await_bank(act, "sv_rows", i)
                if i < QB:
                    copy(sv_tok[:, i, :], src[:, :]).then_inc(read["TR"], 1)
                else:
                    copy(vd_row[:, 0:512], src[0:NB, :]).then_inc(read["TR"], 1)

            def dv_rows(n):
                g, r = n // 3, n % 3
                src = await_bank(act, "dv_rows", n)
                if r < 2:
                    copy(dv_tok[:, 2 * r:2 * r + 2, 256 * g:256 * g + 256],
                         src[:, :].rearrange("p (i c) -> p i c", i=2)).then_inc(read["TR"], 1)
                else:
                    act.wait_ge(vdrow_out, 16)
                    copy(vd_row[:, 256 * g:256 * g + 256], src[0:NB, 0:256]).then_inc(read["TR"], 1)

            def p_weights(n):
                i, h = n // SBH, n % SBH
                keys = slice(0, P * (i + 1))
                src = await_bank(act, "p_scores", n)
                z, l = pz[:, n % 2, keys], psp[:, n % 2, keys]
                nc.scalar.activation(z, src[:, keys], ACT.Identity, scale=SCALE,
                                     bias=bsb[:, h:h + 1]).then_inc(of(read, "p_scores", n), 1)
                await_taken(act, "p_scores", n)
                link(nc.scalar.activation(l, z, ACT.Abs))
                link(nc.scalar.activation(l, l, ACT.Exp, scale=-1.0))
                nc.scalar.activation(l, l, ACT.Ln, bias=1.0).then_inc(p_lnmade, 1)

            def p_turn(n):
                w_ = pw[:, n % 2, 0:P * (n // SBH + 1)]
                act.wait_ge(p_wmade, n + 1)
                nc.scalar.activation(w_, w_, ACT.Exp, scale=-1.0).then_inc(p_amade, 1)

            def p_sum(n):
                if n % SBH == SBH - 1:
                    copy(o_tok[:], await_bank(act, "p_sum", n // SBH)[:, :]).then_inc(read["OU"], 1)

            def p_out(i):
                copy(o_sbT[:, :, P * i:P * i + P],
                     await_bank(act, "p_out", i)[:, :].rearrange("p (t q) -> p t q", t=4)).then_inc(read["TR"], 1)

            def d_softplus(b):
                act.wait_ge(d_made, b + 1)
                link(nc.scalar.activation(de[:], dz[:], ACT.Abs))
                link(nc.scalar.activation(de[:], de[:], ACT.Exp, scale=-1.0))
                nc.scalar.activation(de[:], de[:], ACT.Ln, bias=1.0).then_inc(d_ln, 1)

            def d_weights(b):
                await_taken(act, "d_suffix", b)
                nc.scalar.activation(dw[:, b % 2], dw[:, b % 2], ACT.Exp, scale=-1.0).then_inc(dec_made, 1)

            def d_out(_):
                act.wait_ge(v_used, NKB)
                for e in range(2):
                    rows = slice(HD * e, HD * e + HD)
                    copy(o_sbT[rows, :, S:TOK], dec_sum[rows, :, :, e].rearrange("p b t -> p t b")).then_inc(o_made, 1)

            def phase(n):
                nc.scalar.drain().then_inc(phase_reached, 1)
                act.wait_ge(phase_reached, 4 * n)

            def l_weights(n):
                j, i = n // QB, n % QB
                act.wait_ge(l_made, n + 1)
                logits = lg[:, n % 2, 0:n_keys(i)[2]]
                nc.scalar.activation(logits, logits, ACT.Exp, bias=stat[:, n % 2, 4:5],
                                     accum_out=stat[:, j % 2, i:i + 1]).then_inc(l_pmade, 1)

            def l_sum(n):
                for g in range(NG):
                    cols = n_keys(n % QB)[1 if g == 0 else 0]
                    src = await_bank(act, "l_turn", n, g)
                    copy(lT[:, (NG * n + g) % 2, 0:cols], src[:, 0:cols]).then_inc(read["TR"], 1)

            def l_out(t):
                copy(o_dT[:, t, 0:S], await_bank(act, "l_out", t)[:, :]).then_inc(read["TR"], 1)

            def conv_state(_):
                copy(stT[:].rearrange("p t b k -> p (t b k)"),
                     await_bank(act, "conv_state", 0)[:, 0:64]).then_inc(read["TR"], 1)

            def s_rows(_):
                for r in range(4):
                    dst = (qd_row, kd_row)[r // 2]
                    c, n = ((0, 512), (512, 256))[r % 2]
                    copy(dst[:, c:c + n], await_bank(act, "s_rows", r)[0:NB, 0:n]).then_inc(read["TR"], 1)

            def s_turn(g):
                copy(slog[:, :, g, 0:P],
                     await_bank(act, "s_turn", g)[0:NB, :].rearrange("b (h i) -> b h i", h=GH)).then_inc(read["TR"], 1)

            def s_soft(_):
                act.wait_ge(s_zmade, 1)
                flat = slog[:].rearrange("b h g i -> b (h g i)")
                nc.scalar.activation(flat, flat, ACT.Exp).then_inc(s_pmade, 1)

            def s_back(_):
                copy(spT[:].rearrange("p g h b -> p (g h b)"),
                     await_bank(act, "s_back", 0)[:, 0:NG * GH * NB]).then_inc(read["TR"], 1)

            def s_sum(_):
                src = await_bank(act, "s_sum")
                halves = src[:, 0:2 * 2 * NB].rearrange("p (t e b) -> p t e b", t=2, e=2)
                link(copy(o_dT[0:HD, :, S:TOK], halves[0:HD, :, 0, :]))
                copy(o_dT[HD:P, :, S:TOK], halves[HD:P, :, 1, :]).then_inc(read["OU"], 1)

            def branch_split(_):
                for src, t, n in ((convy, 0, 4), (o_sbT, 4, 4), (o_dT, 8, 2)):
                    copy(binh[:, t:t + n, :], src[:]).then_inc(bin_hi, 1)

            def x_turn(t):
                copy(hT[:, t, 0:S], await_bank(act, "x_turn", t, "prompt")[:, :]).then_inc(read["TR"], 1)
                copy(hT[:, t, S:TOK], await_bank(act, "x_turn", t, "sample")[:, 0:NB]).then_inc(read["OU"], 1)

            def mix_split(tile):
                act.wait_ge(mix_ready, 2 * tile + 2)
                copy(mixh[:, tile, :], macc[:, tile % 2, :], scale=0.5).then_inc(mix_hi, 1)

            def h_ready_tile(t):
                act.wait_ge(dve_took, EVAC[at("out", t)][1])
                if t:
                    act.wait_ge(hacc_made, t)
                nc.scalar.activation(h2[:], hT[:, t, :], ACT.Square).then_inc(h2_made, 1)
                act.wait_ge(hn_made, t + 1)
                copy(xh[:, t, :], hn[:, t % 2, :]).then_inc(hn_hi, 1)

            stages = dict(tables=tables, q_rows=q_rows, q_spread=q_spread, sk_rows=sk_rows, dk_rows=dk_rows,
                          conv_rows=conv_rows, sv_rows=sv_rows, dv_rows=dv_rows, p_weights=p_weights,
                          p_turn=p_turn, p_sum=p_sum, p_out=p_out, d_softplus=d_softplus, d_weights=d_weights,
                          d_out=d_out, phase=phase, l_weights=l_weights, l_sum=l_sum, l_out=l_out,
                          conv_state=conv_state, s_rows=s_rows, s_turn=s_turn, s_soft=s_soft, s_back=s_back,
                          s_sum=s_sum, branch_split=branch_split, x_turn=x_turn)
            for k, (u, job, h, last) in enumerate(TICKS):
                tile = SLABS[UNITS[u][0]]["tile"] + UNITS[u][1]
                if EVAC[k][0]:
                    take(k)
                if last and u + 2 < NUNITS:
                    split_hi(u + 2)
                if job[0] == "yc" and h:
                    mix_split(tile)
                for stage, n in PLAN[k]:
                    if stage in stages:
                        stages[stage](n)
                if job[0] == "out" and h:
                    h_ready_tile(tile)

            nc.scalar.drain().then_inc(phase_reached, 1)
            for h in range(2):
                act.wait_ge(var_read, h + 1)
                nc.scalar.activation(rstdb[:, half(h)], rstdb[:, half(h)], ACT.Sqrt).then_inc(sd_made, 1)
            act.wait_ge(made, LAST_TICK[NUNITS - 2] + 1)
            with act.Fori(0, QUARTERS) as q:
                for u in range(2 * MSLABS):
                    if u % 2 == 0:
                        m = u // 2
                        act.wait_ge(m_in_slot[m % MR], 16 * (2 * q + m // MR + 1))
                    act.wait_ge(m_made, 4 * QT * q + 2 * u)
                    copy(whi[:, u % 2], mraw[:, (u // 2) % MR, :, P * (u % 2):P * (u % 2) + P]).then_inc(w_hi, 1)
                    if 1 <= u <= QT:
                        for h in range(2):
                            n = 2 * (u - 1) + h
                            act.wait_ge(m_took, 4 * QT * q + n + 1 + len(MB))
                            if n >= 2:
                                act.wait_ge(hid_lo, 2 * QT * q + n - 1)
                            nc.scalar.activation(msq[:, h], mt[:, h], ACT.Square).then_inc(m_sq, 1)
                            act.wait_ge(m_sq, 2 * QT * q + n + 1)
                            copy(hidh[:, u - 1, half(h)], msq[:, h]).then_inc(hid_hi, 1)

            for i in range(QB + 1):
                rows = slice(0, P if i < QB else NB)
                for c in range(2):
                    act.wait_ge(y_T, 2 * i + c + 1)
                    nc.scalar.activation(yjunk[rows, 512 * c:512 * c + 512], MB[2 * (i % 2) + c][rows, :], ACT.Square,
                                         accum_out=stat[rows, i % 2, c:c + 1]).then_inc(y_sum, 1)
                act.wait_ge(y_sd, i + 1)
                nc.scalar.activation(stat[rows, i % 2, 2:3], stat[rows, i % 2, 2:3], ACT.Sqrt).then_inc(y_rstd, 1)

        @block.vector
        def _(dve):
            done = [0]

            def link(ins):
                done[0] += 1
                ins.then_inc(dve_done, 1)
                dve.wait_ge(dve_done, done[0])

            def tt(out, a, b, op):
                return nc.vector.tensor_tensor(out, a, b, op)

            def stt(out, a, scalar, b, op0, op1):
                return nc.vector.scalar_tensor_tensor(out, a, scalar, b, op0, op1)

            nc.vector.memset(relb[BUCKETS:BUCKETS + 1, :], 1.0).then_inc(consts_made, 1)
            dve.wait_ge(act_done, QB + 1)
            link(nc.vector.tensor_scalar(rms[:, 0:QB], ss[:, 0:QB], 1.0 / D, EPS, ALU.mult, ALU.add))
            link(nc.vector.tensor_scalar(rms[0:NB, QB:QB + 1], ss[0:NB, QB:QB + 1], 1.0 / D, EPS, ALU.mult, ALU.add))
            dve.wait_ge(act_done, QB + 3)
            link(nc.vector.reciprocal(rstd[:, 0:QB], rms[:, 0:QB]))
            link(nc.vector.reciprocal(rstd[0:NB, QB:QB + 1], rms[0:NB, QB:QB + 1]))
            nc.vector.tensor_scalar(nsrow[:], xsrow[:], rstd[0:NB, QB:QB + 1], None, ALU.mult).then_inc(x_scaled, 1)
            for i in range(QB):
                nc.vector.tensor_scalar(nrow[:, i, :], xrow[:, i, :], rstd[:, i:i + 1], None, ALU.mult).then_inc(x_scaled, 1)
            for n in range(2, 5):
                dve.wait_ge(const_in[n], 16)
            nc.vector.tensor_scalar(bgate[:], bgate[:], 0.5, None, ALU.mult).then_inc(bgate_made, 1)
            for n in (0, 1, 5, 6, 7, 8, 9):
                dve.wait_ge(const_in[n], 16)
            cols = xjunk[:, 0:KC * NB].rearrange("p (k b) -> p k b", k=KC)
            src = await_bank(dve, "x_norm", KC)
            tt(cols, src[:, 0:KC * NB].rearrange("p (k b) -> p k b", k=KC),
               gmix[:].unsqueeze(2).to_broadcast([P, KC, NB]), ALU.mult).then_inc(read["TR"], 1)
            dve.wait_ge(xh_made, 1)
            tt(xl[:, :, S:TOK], cols, xh[:, :, S:TOK].bitcast(F32), ALU.subtract).then_inc(xl_made, 1)
            for c in range(KC):
                if c >= 2:
                    dve.wait_ge(xh_made, c)
                src = await_bank(dve, "x_norm", c)
                nc.vector.tensor_scalar(xn[:, c % 2, 0:S], src[:, :], gmix[:, c:c + 1], None,
                                        ALU.mult).then_inc(of(read, "x_norm", c), 1)
                dve.wait_ge(xh_made, c + 2)
                tt(xl[:, c, 0:S], xn[:, c % 2, 0:S], xh[:, c, 0:S].bitcast(F32), ALU.subtract).then_inc(xl_made, 1)

            def take(k):
                u, job, h, last = TICKS[k]
                s, t = UNITS[u]
                kind, tile = job[0], SLABS[s]["tile"] + t
                src = G[k % GBANKS][:, 0:HALF]
                if kind == "ch":
                    dve.wait_ge(act_took, EVAC[at("cc", tile, h)][1])
                    dve.wait_ge(made, k + 1)
                    u_half = convu[:, tile % 2, 2 + h * HALF:2 + h * HALF + HALF]
                    tt(u_half, u_half, src, ALU.mult).then_inc(dve_took, 1)
                    if h:
                        convolve(tile, k)
                elif kind == "cb":
                    dve.wait_ge(conv_made, tile + 1)
                    dve.wait_ge(made, k + 1)
                    y = convy[:, tile, half(h)]
                    tt(y, y, src, ALU.mult).then_inc(dve_took, 1)
                elif kind in ("ya", "yb", "yc"):
                    g = ("ya", "yb", "yc").index(kind)
                    dve.wait_ge(act_took, EVAC[at(f"gate{g}", tile, h)][1])
                    dve.wait_ge(made, k + 1)
                    m = macc[:, t, half(h)]
                    gate = tg[:, g, t, half(h)]
                    if g == 0:
                        stt(m, gate, 1.0, src, ALU.add, ALU.mult).then_inc(dve_took, 1)
                    else:
                        stt(mtmp[:, h], gate, 1.0, src, ALU.add, ALU.mult).then_inc(dve_took, 1)
                        dve.wait_ge(dve_took, EVAC[k][1])
                        add = tt(m, m, mtmp[:, h], ALU.add)
                        if g == 1:
                            link(add)
                        else:
                            add.then_inc(mix_ready, 1)
                    if g == 2 and h:
                        dve.wait_ge(mix_hi, tile + 1)
                        stt(mixl[:, tile, :], macc[:, t, :], 0.5, mixh[:, tile, :].bitcast(F32), ALU.mult,
                            ALU.subtract).then_inc(mix_lo, 1)
                else:
                    await_taken(dve, "x_turn", tile, "prompt")
                    await_taken(dve, "x_turn", tile, "sample")
                    dve.wait_ge(made, k + 1)
                    tt(hT[:, tile, half(h)], hT[:, tile, half(h)], src, ALU.add).then_inc(dve_took, 1)

            def convolve(tile, k):
                if tile == 0:
                    await_taken(dve, "conv_state", 0)
                dve.wait_ge(dve_took, EVAC[k][1])
                seq = convu[:, tile % 2, :]
                y = convy[:, tile, :]
                w0, w1, w2 = (convw[:, r, tile:tile + 1] for r in range(3))
                link(nc.vector.tensor_scalar(y, seq[:, 2:2 + TOK], w2, None, ALU.mult))
                link(stt(y[:, 0:S], seq[:, 1:1 + S], w1, y[:, 0:S], ALU.mult, ALU.add))
                link(stt(y[:, 0:S], seq[:, 0:S], w0, y[:, 0:S], ALU.mult, ALU.add))
                link(stt(y[:, S:TOK], stT[:, tile, :, 1], w1, y[:, S:TOK], ALU.mult, ALU.add))
                link(nc.vector.tensor_copy(utail[:, tile, :], seq[:, S:2 + TOK]))
                stt(y[:, S:TOK], stT[:, tile, :, 0], w0, y[:, S:TOK], ALU.mult, ALU.add).then_inc(conv_made, 1)

            def k_scores(n):
                b, page = n // (PAGES // 2), 2 * (n % (PAGES // 2))
                await_taken(dve, "q_spread", b)
                dve.wait_ge(k_in[n % 2], 32 * (n // 2 + 1))
                if n:
                    dve.wait_ge(z_made, n)
                tt(prod[:], kpg[:, 2 * (n % 2):2 * (n % 2) + 2, :],
                   qs[:, b % 2:b % 2 + 1, :].to_broadcast([P, 2, 512]), ALU.mult).then_inc(k_used, 1)
                dve.wait_ge(k_used, n + 1)
                nc.vector.tensor_reduce(zs[:, b % 2, page:page + 2, :].rearrange("p a h -> p (a h)"),
                                        prod[:].rearrange("p a (h d) -> p (a h) d", d=HD), AX.X,
                                        ALU.add).then_inc(z_made, 1)

            def d_softplus(b):
                dve.wait_ge(z_made, PAGES // 2 * (b + 1))
                stt(dz[:], zs[:, b % 2], SCALE, bsb[:].unsqueeze(1).to_broadcast([P, PAGES, SBH]), ALU.mult,
                    ALU.add).then_inc(d_made, 1)

            def d_suffix(b):
                dve.wait_ge(d_ln, b + 1)
                link(stt(dsp[:], dz[:], 0.0, de[:], ALU.max, ALU.add))
                src, shift = dsp[:], 1
                for r in range(4):
                    dst = dr[:, r % 2]
                    link(tt(dst[:, 0:PAGES - shift, :], src[:, 0:PAGES - shift, :], src[:, shift:PAGES, :], ALU.add))
                    tail = nc.vector.tensor_copy(dst[:, PAGES - shift:PAGES, :], src[:, PAGES - shift:PAGES, :])
                    if r < 3:
                        link(tail)
                    else:
                        tail.then_inc(d_spmade, 1)
                    src, shift = dst, 2 * shift

                src = await_bank(dve, "d_suffix", b)
                tt(dw[:, b % 2].rearrange("p g h -> p (g h)"), src[:, 0:PAGES * SBH],
                   dz[:].rearrange("p g h -> p (g h)"), ALU.subtract).then_inc(of(read, "d_suffix", b), 1)

            def p_weights(n):
                keys = slice(0, P * (n // SBH + 1))
                z, l, w_ = pz[:, n % 2, keys], psp[:, n % 2, keys], pw[:, n % 2, keys]
                dve.wait_ge(p_lnmade, n + 1)
                link(stt(l, z, 0.0, l, ALU.max, ALU.add))
                link(nc.vector.tensor_tensor_scan(w_[:, ::-1], l[:, ::-1], l[:, ::-1], 0.0, ALU.add, ALU.bypass))
                tt(w_, w_, z, ALU.subtract).then_inc(p_wmade, 1)

            def p_turn(n):
                cols = P * (n // SBH + 1)
                nc.vector.tensor_copy(pT[:, 0:cols], await_bank(dve, "p_turn", n)[:, 0:cols]).then_inc(read["TR"], 1)

            def phase(n):
                nc.vector.drain().then_inc(phase_reached, 1)
                dve.wait_ge(phase_reached, 4 * n)
                if n == 1:
                    link(nc.vector.memset(convu[:, :, 0:2], 0.0))

            def l_scores(n):
                j, i = n // QB, n % QB
                full, first, total = n_keys(i)
                dve.wait_ge(bias_in_slot[j % 2], 16 * NG * (j // 2 + 1))
                for g, (col, keys, at_) in enumerate(((0, first, 0), (256, full, first), (768, full, first + full))):
                    src = await_bank(dve, "l_scores", n, g)
                    stt(lg[:, n % 2, at_:at_ + keys], src[:, 0:keys], SCALE, bias[:, j % 2, col:col + keys][:, ::-1],
                        ALU.mult, ALU.add).then_inc(of(read, "l_scores", n, g), 1)
                for g in range(NG):
                    await_taken(dve, "l_scores", n, g)
                nc.vector.tensor_reduce(stat[:, n % 2, 4:5], lg[:, n % 2, 0:total], AX.X, ALU.max,
                                        negate=True).then_inc(l_made, 1)

            def l_sum(n):
                if n % QB < QB - 1:
                    return
                j = n // QB
                src = await_bank(dve, "l_sum", j)
                link(nc.vector.reciprocal(rstd[:, 0:QB], stat[:, j % 2, 0:QB]))
                if j >= 2:
                    await_bank(dve, "l_out", j // 2 - 1)
                tt(o_tok[:].rearrange("p (i c) -> p i c", i=QB)[:, :, HD * (j % 2):HD * (j % 2) + HD],
                   src[:, 0:QB * HD].rearrange("p (i d) -> p i d", i=QB),
                   rstd[:, 0:QB].unsqueeze(2).to_broadcast([P, QB, HD]), ALU.mult).then_inc(read["OU"], 1)

            def s_scores(n):
                g, b = n // 4, 2 * (n % 4)
                if n % 4 == 0:
                    dve.wait_ge(sK_in[g], 16)
                if n:
                    dve.wait_ge(s_Tmade, n)
                src = await_bank(dve, "s_scores", n)
                tt(sprod[:], sK[g][:, b:b + 2, :], src[:, :].rearrange("p (b c) -> p b c", b=2),
                   ALU.mult).then_inc(of(read, "s_scores", n), 1)
                await_taken(dve, "s_scores", n)
                nc.vector.tensor_reduce(sz[:, g, b:b + 2, :].rearrange("p b h -> p (b h)"),
                                        sprod[:].rearrange("p b (h d) -> p (b h) d", d=HD), AX.X,
                                        ALU.add).then_inc(s_Tmade, 1)
                if n % 4 == 3:
                    dve.wait_ge(s_Tmade, n + 1)
                    stt(sz[:, g], sz[:, g], SCALE, stepbias[:, GH * g:GH * g + GH].unsqueeze(1).to_broadcast([P, NB, GH]),
                        ALU.mult, ALU.add).then_inc(s_rowsmade, 1)

            def s_self(_):
                for r in range(4):
                    await_taken(dve, "s_rows", r)
                link(tt(srprod[:], qd_row[:], kd_row[:], ALU.mult))
                link(nc.vector.tensor_reduce(sself[:], srprod[:].rearrange("b (h d) -> b h d", d=HD), AX.X, ALU.add))
                link(stt(slog[:, :, :, P], sself[:].rearrange("b (g h) -> b h g", h=GH), SCALE,
                         selfbias[:].rearrange("b (g h) -> b h g", h=GH), ALU.mult, ALU.add))

            def s_soft(_):
                for g in range(NG):
                    await_taken(dve, "s_turn", g)
                rows = slog[:].rearrange("b h g i -> b h (g i)")
                spread = [NB, GH, NG * (P + 1)]
                link(nc.vector.tensor_reduce(smax[:], rows, AX.X, ALU.max))
                tt(rows, rows, smax[:].unsqueeze(2).to_broadcast(spread), ALU.subtract).then_inc(s_zmade, 1)
                dve.wait_ge(s_pmade, 1)
                link(nc.vector.tensor_reduce(ssum[:], rows, AX.X, ALU.add))
                link(nc.vector.reciprocal(ssum[:], ssum[:]))
                link(tt(rows, rows, ssum[:].unsqueeze(2).to_broadcast(spread), ALU.mult))
                for g in range(NG):
                    tt(spself[:, g], slog[:, :, g, P:P + 1].to_broadcast([NB, GH, NB]),
                       ident[0:NB, 0:NB].unsqueeze(1).to_broadcast([NB, GH, NB]), ALU.mult).then_inc(s_backmade, 1)

            def branch_split(_):
                for n_, (src, t, n) in enumerate(((convy, 0, 4), (o_sbT, 4, 4), (o_dT, 8, 2))):
                    dve.wait_ge(bin_hi, n_ + 1)
                    tt(binl[:, t:t + n, :], src[:], binh[:, t:t + n, :].bitcast(F32), ALU.subtract).then_inc(bin_lo, 1)

            def h_gain(t):
                if t >= 2:
                    dve.wait_ge(hn_hi, t - 1)
                dve.wait_ge(dve_took, EVAC[at("out", t)][1])
                nc.vector.tensor_scalar(hn[:, t % 2, :], hT[:, t, :], gmlp[:, t:t + 1], None, ALU.mult).then_inc(hn_made, 1)

            def h_sum(t):
                dve.wait_ge(h2_made, t + 1)
                if t == 0:
                    nc.vector.tensor_copy(hacc[:], h2[:]).then_inc(hacc_made, 1)
                else:
                    dve.wait_ge(hacc_made, t)
                    tt(hacc[:], hacc[:], h2[:], ALU.add).then_inc(hacc_made, 1)
                dve.wait_ge(hn_hi, t + 1)
                tt(xl[:, t, :], hn[:, t % 2, :], xh[:, t, :].bitcast(F32), ALU.subtract).then_inc(hn_lo, 1)

            stages = dict(k_scores=k_scores, d_softplus=d_softplus, d_suffix=d_suffix,
                          p_weights=p_weights, p_turn=p_turn, phase=phase, l_scores=l_scores, l_sum=l_sum,
                          s_scores=s_scores, s_self=s_self, s_soft=s_soft, branch_split=branch_split)
            for k, (u, job, h, last) in enumerate(TICKS):
                tile = SLABS[UNITS[u][0]]["tile"] + UNITS[u][1]
                if not EVAC[k][0]:
                    take(k)
                for stage, n in PLAN[k]:
                    if stage in stages:
                        stages[stage](n)
                if job[0] == "out" and h:
                    h_gain(tile)
                    if tile:
                        h_sum(tile - 1)
            h_sum(KC - 1)
            nc.vector.drain().then_inc(phase_reached, 1)

            for h in range(2):
                dve.wait_ge(m_made, h + 1)
                nc.vector.tensor_scalar(rstdb[:, half(h)], bank[("TR", "OU")[h]][:, 0:HALF], 1.0 / D, EPS, ALU.mult,
                                        ALU.add).then_inc(var_read, 1)
            for h in range(2):
                dve.wait_ge(sd_made, h + 1)
                link(nc.vector.reciprocal(rstdb[:, half(h)], rstdb[:, half(h)]))
            for i in range(len(MB)):
                nc.vector.memset(mtmp[:, 0, i:i + 1], 0.0).then_inc(m_took, 1)

            def hid_split(q, u):
                for h in range(2):
                    n = 2 * u + h
                    dve.wait_ge(hid_hi, 2 * QT * q + n + 1)
                    tt(hidl[:, u, half(h)], msq[:, h], hidh[:, u, half(h)].bitcast(F32), ALU.subtract).then_inc(hid_lo, 1)

            with dve.Fori(0, QUARTERS) as q:
                for u in range(QT):
                    for h in range(2):
                        n = 2 * u + h
                        dve.wait_ge(m_made, 4 * QT * q + n + 3)
                        if n >= 2:
                            dve.wait_ge(m_sq, 2 * QT * q + n - 1)
                        stt(mt[:, h], MB[n % 4][:, 0:HALF], 0.0, rstdb[:, half(h)], ALU.max, ALU.mult).then_inc(m_took, 1)
                    if u:
                        hid_split(q, u - 1)
                hid_split(q, QT - 1)
                for u in range(KC):
                    for h in range(2):
                        n = 2 * QT + 2 * u + h
                        dve.wait_ge(m_made, 4 * QT * q + n + 3)
                        dve.wait_ge(m_took, 4 * QT * q + len(MB))
                        tt(hT[:, u, half(h)], hT[:, u, half(h)], MB[n % 4][:, 0:HALF], ALU.add).then_inc(m_took, 1)

            dve.wait_ge(gfin_in, 16)
            for i in range(QB + 1):
                rows = slice(0, P if i < QB else NB)
                st = stat[rows, i % 2, :]
                dve.wait_ge(y_sum, 2 * i + 2)
                link(tt(st[:, 3:4], st[:, 0:1], st[:, 1:2], ALU.add))
                nc.vector.tensor_scalar(st[:, 2:3], st[:, 3:4], 1.0 / D, EPS, ALU.mult, ALU.add).then_inc(y_sd, 1)
                dve.wait_ge(y_rstd, i + 1)
                link(nc.vector.reciprocal(st[:, 4:5], st[:, 2:3]))
                if i >= 2:
                    dve.wait_ge(y_out[i % 2], 16 * (i // 2))
                for c in range(2):
                    stt(yrow[rows, i % 2, 512 * c:512 * c + 512], MB[2 * (i % 2) + c][rows, :], st[:, 4:5],
                        gfin[rows, 512 * c:512 * c + 512], ALU.mult, ALU.mult).then_inc(y_made, 1)

        @block.tensor
        def _(pe):
            def mm(out, lhsT, rhs, start, stop, **kw):
                return nc.tensor.matmul(out, lhsT, rhs, start=start, stop=stop, **kw)

            def turn(out, in_, rows=P):
                return nc.tensor.transpose(out, in_, ident[0:rows, 0:rows])

            pe.wait_ge(consts_made, 6)
            pe.wait_ge(x_scaled, 1)
            dst = open_bank(pe, "x_norm", KC)
            for c in range(KC):
                ins = turn(dst[:, NB * c:NB * c + NB], nsrow[:, P * c:P * c + P], NB)
            ins.then_inc(written["TR"], 1)
            pe.wait_ge(x_scaled, 1 + QB)
            for c in range(KC):
                dst = open_bank(pe, "x_norm", c)
                for i in range(QB):
                    ins = turn(dst[:, P * i:P * i + P], nrow[:, i, P * c:P * c + P])
                ins.then_inc(of(written, "x_norm", c), 1)

            def project(k):
                u, (kind, k0, nkc, what), h, last = TICKS[k]
                act_h, act_l, a0 = source[what]
                pe.wait_ge(w_lo, u + 1)
                if kind == "sq" and k < 2:
                    pe.wait_ge(xl_made, 1)
                if k >= GBANKS:
                    pe.wait_ge(*took(k - GBANKS))
                if kind == "ya":
                    pe.wait_ge(bin_lo, 1)
                elif kind == "yb":
                    pe.wait_ge(bin_lo, 2)
                elif kind == "yc":
                    pe.wait_ge(bin_lo, 3)
                elif kind == "out":
                    pe.wait_ge(mix_lo, KC)
                out = G[k % GBANKS][:, 0:HALF]
                for kc in range(nkc):
                    if k == 0:
                        pe.wait_ge(xl_made, kc + 2)
                    wh, wl = whi[:, u % 2, k0 + kc, :], wlo[:, u % 2, k0 + kc, :]
                    ah, al = act_h[:, a0 + kc, half(h)], act_l[:, a0 + kc, half(h)]
                    mm(out, wh, ah, kc == 0, False)
                    mm(out, wh, al, False, False)
                    ins = mm(out, wl, ah, False, kc == nkc - 1)
                ins.then_inc(made, 1)

            def tables(_):
                pe.wait_ge(const_in[10], 16)
                pe.wait_ge(hot_in, 16)
                pe.wait_ge(hots_in, 16)
                for g in range(NG):
                    for part, (c, n) in enumerate(((0, 512), (512, NU + 1 - 512))):
                        dst = open_bank(pe, "table", g, part)
                        mm(dst[0:GH, 0:n], relb[:, GH * g:GH * g + GH], hot[:, g, c:c + n], True,
                           True).then_inc(of(written, "table", g, part), 1)
                dst = open_bank(pe, "table_s")
                for g in range(NG):
                    ins = mm(dst[:, GH * g:GH * g + GH], hots[:, g, :], relb[0:BUCKETS, GH * g:GH * g + GH], True, True)
                ins.then_inc(of(written, "table_s"), 1)

            def rows_of(stage, n, srcs, rows):
                dst = open_bank(pe, stage, n)
                for t, src in enumerate(srcs):
                    ins = turn(dst[0:rows, P * t:P * t + P], src)
                ins.then_inc(of(written, stage, n), 1)

            def tokens(i):
                return slice(P * i, P * i + P) if i < QB else slice(S, TOK)

            def n_tokens(i):
                return P if i < QB else NB

            def q_rows(_):
                pe.wait_ge(act_took, EVAC[at("sq", 3)][1])
                rows_of("q_rows", 0, [sqT[:, t, S:TOK] for t in range(4)], NB)

            def q_spread(b):
                await_taken(pe, "q_rows", 0)
                dst = open_bank(pe, "q_spread", b)
                mm(dst[:, :], ident[0:NB, b:b + 1].to_broadcast([NB, P]), q_row[:], True,
                   True).then_inc(of(written, "q_spread", b), 1)

            def sk_rows(i):
                pe.wait_ge(act_took, EVAC[at("sk", 3)][1])
                rows_of("sk_rows", i, [skT[:, t, tokens(i)] for t in range(4)], n_tokens(i))

            def sv_rows(i):
                pe.wait_ge(act_took, EVAC[at("sv", 3)][1])
                rows_of("sv_rows", i, [svT[:, t, tokens(i)] for t in range(4)], n_tokens(i))

            def dk_rows(n):
                i, part = n // 2, n % 2
                pe.wait_ge(act_took, EVAC[at("dk", 5)][1])
                rows_of("dk_rows", n, [dkT[:, t, tokens(i)] for t in ((0, 1, 2, 3) if part == 0 else (4, 5))], n_tokens(i))

            def dv_rows(n):
                g, r = n // 3, n % 3
                pe.wait_ge(act_took, EVAC[at("dv", 2 * g + 1)][1])
                blocks = (2 * r, 2 * r + 1) if r < 2 else (QB,)
                rows_of("dv_rows", n, [dvT[:, g % 2, t, tokens(i)] for i in blocks for t in range(2)], n_tokens(blocks[0]))

            def p_scores(n):
                i, (t, rows) = n // SBH, head(n % SBH)
                keys = P * (i + 1)
                if n == 0:
                    pe.wait_ge(act_took, EVAC[at("sk", 3)][1])
                dst = open_bank(pe, "p_scores", n)
                mm(dst[:, 0:keys], sqT[rows, t, P * i:P * i + P], skT[rows, t, 0:keys], True, False)
                mm(dst[:, keys - P:keys], identb[:], maskb[:], False, True).then_inc(of(written, "p_scores", n), 1)

            def p_turn(n):
                pe.wait_ge(p_amade, n + 1)
                dst = open_bank(pe, "p_turn", n)
                for b in range(n // SBH + 1):
                    ins = turn(dst[:, P * b:P * b + P], pw[:, n % 2, P * b:P * b + P])
                ins.then_inc(written["TR"], 1)

            def p_sum(n):
                i, h = n // SBH, n % SBH
                await_taken(pe, "p_turn", n)
                await_taken(pe, "sv_rows", i)
                dst = open_bank(pe, "p_sum", i) if h == 0 else bank["OU"]
                for b in range(i + 1):
                    ins = mm(dst[:, HD * h:HD * h + HD], pT[:, P * b:P * b + P], sv_tok[:, b, HD * h:HD * h + HD],
                             b == 0, b == i)
                if h == SBH - 1:
                    ins.then_inc(written["OU"], 1)

            def p_out(i):
                await_taken(pe, "p_sum", i)
                rows_of("p_out", i, [o_tok[:, P * t:P * t + P] for t in range(4)], P)

            def d_suffix(b):
                pe.wait_ge(d_spmade, b + 1)
                dst = open_bank(pe, "d_suffix", b)
                mm(dst[:, 0:PAGES * SBH], tri[:], dsp[:].rearrange("p g h -> p (g h)"), True, False)
                mm(dst[:, 0:(PAGES - 1) * SBH], ones[:], dr[:, 1, 1:PAGES, :].rearrange("p g h -> p (g h)"), False,
                   True).then_inc(of(written, "d_suffix", b), 1)

            def v_sum(n):
                b = n // (PAGES // 2)
                pe.wait_ge(dec_made, b + 1)
                pe.wait_ge(v_in[n % 2], 32 * (n // 2 + 1))
                for p in range(2):
                    page = 2 * (n % (PAGES // 2)) + p
                    for t in range(4):
                        ins = mm(dec_sum[:, b, t, :], vpg[:, 2 * (n % 2) + p, P * t:P * t + P],
                                 dw[:, b % 2, page, 2 * t:2 * t + 2], n == 0 and p == 0 and t == 0,
                                 page == PAGES - 1, skip_group_check=True)
                ins.then_inc(v_used, 1)

            def phase(n):
                nc.tensor.drain().then_inc(phase_reached, 1)
                pe.wait_ge(phase_reached, 4 * n)

            def conv_state(_):
                pe.wait_ge(st_in, 16)
                dst = open_bank(pe, "conv_state", 0)
                for t in range(4):
                    ins = turn(dst[:, 2 * NB * t:2 * NB * t + 2 * NB], st_row[:, P * t:P * t + P], 2 * NB)
                ins.then_inc(written["TR"], 1)

            def conv_rows(_):
                pe.wait_ge(conv_made, 4)
                rows_of("conv_rows", 0, [utail[:, t, :] for t in range(4)], 2 + NB)

            def l_scores(n):
                j, i = n // QB, n % QB
                full, first, _ = n_keys(i)
                if n == 0:
                    pe.wait_ge(act_took, EVAC[at("dk", 5)][1])
                for g in range(NG):
                    t, rows = head(GH * g + j)
                    k0 = full - first if g == 0 else 0
                    dst = open_bank(pe, "l_scores", n, g)
                    mm(dst[:, 0:full - k0], dqT[rows, t, P * i:P * i + P], dkT[rows, t, k0:full], True,
                       True).then_inc(of(written, "l_scores", n, g), 1)

            def l_sum(n):
                j, i = n // QB, n % QB
                full, first, _ = n_keys(i)
                widths = (first, full, full)
                pe.wait_ge(l_pmade, n + 1)
                if n == 0:
                    for m in (0, 1, 3, 4, 6, 7):
                        await_taken(pe, "dv_rows", m)
                if i == 0:
                    open_bank(pe, "l_sum", j)
                out = bank["OU"][:, HD * i:HD * i + HD]

                def turn_group(g):
                    dst = open_bank(pe, "l_turn", n, g)
                    c0 = sum(widths[0:g])
                    for c in range(0, widths[g], P):
                        ins = turn(dst[:, c:c + P], lg[:, n % 2, c0 + c:c0 + c + P])
                    ins.then_inc(written["TR"], 1)

                def sum_group(g):
                    await_taken(pe, "l_turn", n, g)
                    blocks = widths[g] // P
                    for c in range(blocks):
                        kb = i + 1 - blocks + c
                        last = g == NG - 1 and c == blocks - 1
                        ins = mm(out, lT[:, (NG * n + g) % 2, P * c:P * c + P],
                                 dv_tok[:, kb, 256 * g + HD * j:256 * g + HD * j + HD], g == 0 and c == 0, last)
                    if last and i == QB - 1:
                        ins.then_inc(written["OU"], 1)

                turn_group(0)
                turn_group(1)
                sum_group(0)
                turn_group(2)
                sum_group(1)
                sum_group(2)

            def l_out(t):
                await_taken(pe, "l_sum", 2 * t)
                await_taken(pe, "l_sum", 2 * t + 1)
                rows_of("l_out", t, [o_tok[:, P * i:P * i + P] for i in range(QB)], P)

            def s_rows(_):
                for r in range(4):
                    src = (dqT, dkT)[r // 2]
                    dst = open_bank(pe, "s_rows", r)
                    for c, t in enumerate(((0, 1, 2, 3), (4, 5))[r % 2]):
                        ins = turn(dst[0:NB, P * c:P * c + P], src[:, t, S:TOK])
                    ins.then_inc(written["TR"], 1)

            def s_scores(n):
                g, b = n // 4, 2 * (n % 4)
                await_taken(pe, "s_rows", 1)
                dst = open_bank(pe, "s_scores", n)
                for e in range(2):
                    ins = mm(dst[:, 256 * e:256 * e + 256], ident[0:NB, b + e:b + e + 1].to_broadcast([NB, P]),
                             qd_row[:, 256 * g:256 * g + 256], True, True)
                ins.then_inc(of(written, "s_scores", n), 1)

            def s_turn(g):
                pe.wait_ge(s_rowsmade, g + 1)
                dst = open_bank(pe, "s_turn", g)
                for h in range(GH):
                    ins = turn(dst[0:NB, P * h:P * h + P], sz[:, g, :, h])
                ins.then_inc(written["TR"], 1)

            def s_back(_):
                pe.wait_ge(s_backmade, NG)
                dst = open_bank(pe, "s_back", 0)
                for g in range(NG):
                    for h in range(GH):
                        c = (GH * g + h) * NB
                        ins = turn(dst[:, c:c + NB], slog[:, h, g, 0:P], NB)
                ins.then_inc(written["TR"], 1)

            def s_sum(_):
                for m in (2, 5, 8):
                    await_taken(pe, "dv_rows", m)
                await_taken(pe, "s_back", 0)
                for g in range(NG):
                    pe.wait_ge(sV_in[g], 16)
                dst = open_bank(pe, "s_sum")
                for t in range(2):
                    out = dst[:, 2 * NB * t:2 * NB * t + 2 * NB]
                    for g in range(NG):
                        cols = slice(256 * g + P * t, 256 * g + P * t + P)
                        mm(out, vd_row[:, cols], spself[:, g, 2 * t:2 * t + 2, :].rearrange("b e c -> b (e c)"),
                           g == 0, False, skip_group_check=True)
                    pairs = out.rearrange("p (e b) -> p e b", e=2)
                    for g in range(NG):
                        for b in range(NB):
                            ins = mm(pairs[:, :, b], sV[g][:, b, P * t:P * t + P], spT[:, g, 2 * t:2 * t + 2, b], False,
                                     g == NG - 1, skip_group_check=True)
                ins.then_inc(written["OU"], 1)

            def x_turn(t):
                pe.wait_ge(xa_in, 32)
                dst = open_bank(pe, "x_turn", t, "prompt")
                for i in range(QB):
                    ins = turn(dst[:, P * i:P * i + P], xarow[:, i, P * t:P * t + P])
                ins.then_inc(written["TR"], 1)
                dst = open_bank(pe, "x_turn", t, "sample")
                turn(dst[:, 0:NB], xasrow[:, P * t:P * t + P], NB).then_inc(written["OU"], 1)

            stages = dict(tables=tables, q_rows=q_rows, q_spread=q_spread, sk_rows=sk_rows, sv_rows=sv_rows,
                          dk_rows=dk_rows, dv_rows=dv_rows, p_scores=p_scores, p_turn=p_turn, p_sum=p_sum,
                          p_out=p_out, d_suffix=d_suffix, v_sum=v_sum, phase=phase, conv_state=conv_state,
                          conv_rows=conv_rows, l_scores=l_scores, l_sum=l_sum, l_out=l_out, s_rows=s_rows,
                          s_scores=s_scores, s_turn=s_turn, s_back=s_back, s_sum=s_sum, x_turn=x_turn)
            for k in range(NT):
                project(k)
                for stage, n in PLAN[k]:
                    if stage in stages:
                        stages[stage](n)
            nc.tensor.drain().then_inc(phase_reached, 1)

            pe.wait_ge(hacc_made, KC)
            pe.wait_ge(hn_lo, KC)
            for h, name in enumerate(("TR", "OU")):
                pe.wait_ge(read[name], len(USES[name]))
                mm(bank[name][:, 0:HALF], ones[:], hacc[:, half(h)], True, True).then_inc(m_made, 1)
            pe.wait_ge(dve_took, EVAC[NT - 1][1])
            pe.wait_ge(read["S0"], len(USES["S0"]))
            with pe.Fori(0, QUARTERS) as q:
                for u in range(2 * QT):
                    pe.wait_ge(w_lo, NUNITS + 2 * QT * q + u + 1)
                    for h in range(2):
                        n = 2 * u + h
                        pe.wait_ge(m_took, 4 * QT * q + n + 1)
                        act_h, act_l = (xh, xl) if u < QT else (hidh, hidl)
                        for kc in range(KC):
                            if u == QT:
                                pe.wait_ge(hid_lo, 2 * QT * q + 2 * kc + h + 1)
                            wh, wl = whi[:, u % 2, kc, :], wlo[:, u % 2, kc, :]
                            ah, al = act_h[:, kc, half(h)], act_l[:, kc, half(h)]
                            out = MB[n % 4][:, 0:HALF]
                            mm(out, wh, ah, kc == 0, False)
                            mm(out, wh, al, False, False)
                            ins = mm(out, wl, ah, False, kc == KC - 1)
                        ins.then_inc(m_made, 1)

            pe.wait_ge(m_took, 4 * QT * QUARTERS + len(MB))
            for i in range(QB + 1):
                if i >= 2:
                    pe.wait_ge(y_made, 2 * (i - 1))
                for c in range(2):
                    dst = MB[2 * (i % 2) + c]
                    for t in range(4):
                        ins = turn(dst[0:n_tokens(i), P * t:P * t + P], hT[:, 4 * c + t, tokens(i)])
                    ins.then_inc(y_T, 1)


INPUTS = ("x_prompt", "x_sample", "cache_sb_k", "cache_sb_v", "cache_win128_k", "cache_win128_v", "cache_win512_k",
          "cache_win512_v", "cache_win2048_k", "cache_win2048_v", "state_conv", "page_table", "norm_mix_g", "w_in",
          "b_gate", "conv_w", "w_branch_conv", "w_branch_sb", "b_sb", "w_branch_dil", "w_out", "norm_mlp_g",
          "w_mlp_up", "w_mlp_down", "rel_bias", "norm_final_g")


def output_shapes():
    shapes = {"y_prompt": (1, S, D), "y_sample": (NB, 1, D),
              "sb_k_prompt": (1, 1, S, SBH, HD), "sb_v_prompt": (1, 1, S, SBH, HD),
              "sb_k_sample": (1, NB, 1, SBH, HD), "sb_v_sample": (1, NB, 1, SBH, HD)}
    for window, _ in DIL:
        for kind in "kv":
            shapes[f"win{window}_{kind}_prompt"] = (1, 1, min(window, S), GH, HD)
    for window, _ in DIL:
        for kind in "kv":
            shapes[f"win{window}_{kind}_sample"] = (1, NB, window, GH, HD)
    shapes["conv_prompt"] = (1, 1, 2, 512)
    shapes["conv_sample"] = (1, NB, 2, 512)
    return shapes


def kernel(**inputs):
    import concourse.bacc as bacc
    from concourse.bass_utils import run_bass_kernel_spmd

    nc = bacc.Bacc("TRN2", target_bir_lowering=False, num_devices=1)
    arrays, x, o = {}, {}, {}
    hot, hots = bucket_tables()
    for name, a in [(n, inputs[n]) for n in INPUTS] + [("hot", hot), ("hots", hots)]:
        a = np.ascontiguousarray(a)
        arrays[f"in_{name}_dram"] = a
        x[name] = nc.dram_tensor(f"in_{name}_dram", a.shape, mybir.dt.from_np(a.dtype), kind="ExternalInput").ap()
    for name, shape in output_shapes().items():
        o[name] = nc.dram_tensor(f"out_{name}_dram", shape, F32, kind="ExternalOutput").ap()
    w = {"btab": nc.dram_tensor("bias_table_dram", (GH, NG, NU + 1), F32, kind="Internal").ap()}
    decoder_step(nc, x, o, w)
    r = run_bass_kernel_spmd(nc, [arrays], core_ids=[0])
    return tuple(r.results[0][f"out_{name}_dram"] for name in o)
```
